# Optimizing a Trainium2 kernel written in Bass

```python
import math
import jax
import jax.numpy as jnp
from jax import lax
import numpy as np

D_MODEL = 1024
BATCH = 1
SEQ = 1024
DEPTH = 1

N_META = 16
SSM_WIDTH = D_MODEL // 2
SSM_GROUP = 16
SSM_GROUPS = SSM_WIDTH // SSM_GROUP
SSM_STATE = 64
HEAD_DIM = 64
N_HEADS = D_MODEL // HEAD_DIM
N_KV_HEADS = 2
KV_REP = N_HEADS // N_KV_HEADS
WINDOW = 128
ATTN_BLOCK = 128
Q_WIDTH = N_HEADS * HEAD_DIM
KV_WIDTH = N_KV_HEADS * HEAD_DIM
IN_WIDTH = SSM_WIDTH + Q_WIDTH + 2 * KV_WIDTH + 2 * D_MODEL
N_EXPERTS = 32
TOP_K = 4
D_FF = D_MODEL
SWIGLU_ALPHA = 1.702
SWIGLU_LIMIT = 7.0
MOE_BLOCK = 128
RMS_EPS = 1e-5
NEG_INF = -1e30

kernel_name = "hybrid_s5_swa_sink_moe_meta"

def rms_norm(x, g):
    xf = x.astype(jnp.float32)
    y = xf * lax.rsqrt(jnp.mean(xf * xf, axis=-1, keepdims=True) + RMS_EPS)
    return (y * g.astype(jnp.float32)).astype(x.dtype)

def s5_mixer(u, a_re, a_im, log_dt, b_re, b_im, c_re, c_im, d_skip):
    bsz, seq_len, _ = u.shape
    f32 = jnp.float32
    uf = u.astype(f32)
    ug = uf.reshape(bsz, seq_len, SSM_GROUPS, SSM_GROUP)
    a_re, a_im = a_re.astype(f32), a_im.astype(f32)
    b_re, b_im = b_re.astype(f32), b_im.astype(f32)
    c_re, c_im = c_re.astype(f32), c_im.astype(f32)
    dt = jnp.exp(log_dt.astype(f32))[:, None]
    mag = jnp.exp(a_re * dt)
    ang = a_im * dt
    abar_re, abar_im = mag * jnp.cos(ang), mag * jnp.sin(ang)
    den = a_re * a_re + a_im * a_im
    nr, ni = abar_re - 1.0, abar_im
    coef_re = ((nr * a_re + ni * a_im) / den)[..., None]
    coef_im = ((ni * a_re - nr * a_im) / den)[..., None]
    bbar_re = coef_re * b_re - coef_im * b_im
    bbar_im = coef_re * b_im + coef_im * b_re
    bu_re = jnp.einsum('blgc,gpc->blgp', ug, bbar_re)
    bu_im = jnp.einsum('blgc,gpc->blgp', ug, bbar_im)
    ar = jnp.broadcast_to(abar_re[None, None], (1, seq_len, SSM_GROUPS, SSM_STATE))
    ai = jnp.broadcast_to(abar_im[None, None], (1, seq_len, SSM_GROUPS, SSM_STATE))

    def combine(e1, e2):
        a1r, a1i, b1r, b1i = e1
        a2r, a2i, b2r, b2i = e2
        return (a2r * a1r - a2i * a1i,
                a2r * a1i + a2i * a1r,
                a2r * b1r - a2i * b1i + b2r,
                a2r * b1i + a2i * b1r + b2i)

    _, _, s_re, s_im = lax.associative_scan(combine, (ar, ai, bu_re, bu_im), axis=1)
    y = jnp.einsum('blgp,gcp->blgc', s_re, c_re) - jnp.einsum('blgp,gcp->blgc', s_im, c_im)
    y = y.reshape(bsz, seq_len, SSM_WIDTH) + d_skip.astype(f32) * uf
    return y.astype(u.dtype)

def window_attention(q, k, v, sinks):
    bsz, seq_len = q.shape[:2]
    s_real = seq_len - N_META
    nb = s_real // ATTN_BLOCK
    scale = HEAD_DIM ** -0.5
    f32 = jnp.float32
    q = q.reshape(bsz, seq_len, N_KV_HEADS, KV_REP, HEAD_DIM)
    qm, qr = q[:, :N_META], q[:, N_META:]
    km, kr = k[:, :N_META], k[:, N_META:]
    vm, vr = v[:, :N_META], v[:, N_META:]
    sink = sinks.astype(f32).reshape(N_KV_HEADS, KV_REP)

    s_mm = jnp.einsum('bqkrd,bmkd->bkrqm', qm, km).astype(f32) * scale
    causal = jnp.arange(N_META)[:, None] >= jnp.arange(N_META)[None, :]
    s_mm = jnp.where(causal, s_mm, NEG_INF)
    sink_m = jnp.broadcast_to(sink[None, :, :, None, None], (bsz, N_KV_HEADS, KV_REP, N_META, 1))
    p_mm = jax.nn.softmax(jnp.concatenate([s_mm, sink_m], axis=-1), axis=-1)[..., :N_META]
    out_m = jnp.einsum('bkrqm,bmkd->bqkrd', p_mm.astype(v.dtype), vm)

    qb = qr.reshape(bsz, nb, ATTN_BLOCK, N_KV_HEADS, KV_REP, HEAD_DIM)

    def band(t):
        tp = jnp.pad(t, ((0, 0), (ATTN_BLOCK, 0), (0, 0), (0, 0)))
        tp = tp.reshape(bsz, nb + 1, ATTN_BLOCK, N_KV_HEADS, HEAD_DIM)
        return jnp.concatenate([tp[:, :-1], tp[:, 1:]], axis=2)

    kb, vb = band(kr), band(vr)
    s_band = jnp.einsum('bnqkrd,bnskd->bnkrqs', qb, kb).astype(f32) * scale
    qpos = jnp.arange(nb)[:, None, None] * ATTN_BLOCK + jnp.arange(ATTN_BLOCK)[None, :, None]
    kpos = (jnp.arange(nb)[:, None, None] - 1) * ATTN_BLOCK + jnp.arange(2 * ATTN_BLOCK)[None, None, :]
    rel = qpos - kpos
    vis = (rel >= 0) & (rel < WINDOW) & (kpos >= 0)
    s_band = jnp.where(vis[None, :, None, None], s_band, NEG_INF)
    s_meta = jnp.einsum('bnqkrd,bmkd->bnkrqm', qb, km).astype(f32) * scale
    sink_r = jnp.broadcast_to(sink[None, None, :, :, None, None],
                              (bsz, nb, N_KV_HEADS, KV_REP, ATTN_BLOCK, 1))
    p = jax.nn.softmax(jnp.concatenate([s_meta, s_band, sink_r], axis=-1), axis=-1).astype(v.dtype)
    out_r = (jnp.einsum('bnkrqm,bmkd->bnqkrd', p[..., :N_META], vm)
             + jnp.einsum('bnkrqs,bnskd->bnqkrd', p[..., N_META:N_META + 2 * ATTN_BLOCK], vb))
    out_r = out_r.reshape(bsz, s_real, N_KV_HEADS, KV_REP, HEAD_DIM)
    out = jnp.concatenate([out_m, out_r], axis=1)
    return out.reshape(bsz, seq_len, Q_WIDTH)

def clamped_swiglu(x_glu, x_lin):
    x_glu = jnp.minimum(x_glu, SWIGLU_LIMIT)
    x_lin = jnp.clip(x_lin, -SWIGLU_LIMIT, SWIGLU_LIMIT)
    return x_glu * jax.nn.sigmoid(SWIGLU_ALPHA * x_glu) * (x_lin + 1.0)

def moe_ffn(h, router_w, router_b, w_up, b_up, w_down, b_down):
    n_tok = h.shape[0]
    n_assign = n_tok * TOP_K
    logits = (h @ router_w + router_b).astype(jnp.float32)
    top_vals, top_idx = lax.top_k(logits, TOP_K)
    gates = jax.nn.softmax(top_vals, axis=-1)
    e_flat = top_idx.reshape(-1)
    tok_flat = jnp.repeat(jnp.arange(n_tok, dtype=jnp.int32), TOP_K)
    g_flat = gates.reshape(-1)
    order = jnp.argsort(e_flat)
    e_s, tok_s, g_s = e_flat[order], tok_flat[order], g_flat[order]
    counts = jnp.bincount(e_flat, length=N_EXPERTS)
    padded = ((counts + MOE_BLOCK - 1) // MOE_BLOCK) * MOE_BLOCK
    start = jnp.cumsum(counts) - counts
    block_end = jnp.cumsum(padded)
    pstart = block_end - padded
    dest = pstart[e_s] + (jnp.arange(n_assign) - start[e_s])
    n_blocks = (n_assign + N_EXPERTS * (MOE_BLOCK - 1) + MOE_BLOCK - 1) // MOE_BLOCK
    n_rows = n_blocks * MOE_BLOCK
    row_tok = jnp.zeros((n_rows,), jnp.int32).at[dest].set(tok_s)
    row_g = jnp.zeros((n_rows,), jnp.float32).at[dest].set(g_s)
    block_expert = jnp.minimum(
        jnp.searchsorted(block_end, jnp.arange(n_blocks) * MOE_BLOCK, side='right'), N_EXPERTS - 1)

    def expert_block(args):
        tok, e = args
        xb = h[tok]
        up = xb @ w_up[e] + b_up[e]
        act = clamped_swiglu(up[:, :D_FF], up[:, D_FF:])
        return act @ w_down[e] + b_down[e]

    y = lax.map(expert_block, (row_tok.reshape(n_blocks, MOE_BLOCK), block_expert))
    y = y.reshape(n_rows, -1) * row_g[:, None].astype(h.dtype)
    return jax.ops.segment_sum(y, row_tok, num_segments=n_tok)

def setup_inputs(seed: int = 0) -> dict:
    key = jax.random.key(seed)
    ks = jax.random.split(key, 24)
    f32 = jnp.float32
    nrm = lambda k, shape, s: jax.random.normal(k, shape, f32) * s
    x = jax.random.normal(ks[0], (BATCH, SEQ, D_MODEL), f32)
    meta_tokens = nrm(ks[1], (N_META, D_MODEL), 1.0)
    mix_norm_g = 1.0 + nrm(ks[2], (DEPTH, D_MODEL), 0.05)
    w_in = nrm(ks[3], (DEPTH, D_MODEL, IN_WIDTH), D_MODEL ** -0.5)
    ssm_a_re = -0.5 * jnp.exp(nrm(ks[4], (DEPTH, SSM_GROUPS, SSM_STATE), 0.02))
    ssm_a_im = jnp.broadcast_to(math.pi * jnp.arange(SSM_STATE, dtype=f32),
                                (DEPTH, SSM_GROUPS, SSM_STATE))
    ssm_log_dt = jax.random.uniform(ks[5], (DEPTH, SSM_GROUPS), f32,
                                    math.log(0.001), math.log(0.1))
    ssm_b_re = nrm(ks[6], (DEPTH, SSM_GROUPS, SSM_STATE, SSM_GROUP), (2 * SSM_GROUP) ** -0.5)
    ssm_b_im = nrm(ks[7], (DEPTH, SSM_GROUPS, SSM_STATE, SSM_GROUP), (2 * SSM_GROUP) ** -0.5)
    ssm_c_re = nrm(ks[8], (DEPTH, SSM_GROUPS, SSM_GROUP, SSM_STATE), (2 * SSM_STATE) ** -0.5)
    ssm_c_im = nrm(ks[9], (DEPTH, SSM_GROUPS, SSM_GROUP, SSM_STATE), (2 * SSM_STATE) ** -0.5)
    ssm_d = nrm(ks[10], (DEPTH, SSM_WIDTH), 1.0)
    w_ssm_glu = nrm(ks[11], (DEPTH, SSM_WIDTH, 2 * D_MODEL), SSM_WIDTH ** -0.5)
    attn_sinks = nrm(ks[12], (DEPTH, N_HEADS), 0.5)
    w_attn_o = nrm(ks[13], (DEPTH, Q_WIDTH, D_MODEL), Q_WIDTH ** -0.5)
    w_out = nrm(ks[14], (DEPTH, D_MODEL, D_MODEL), D_MODEL ** -0.5)
    ffn_norm_g = 1.0 + nrm(ks[15], (DEPTH, D_MODEL), 0.05)
    router_w = nrm(ks[16], (DEPTH, D_MODEL, N_EXPERTS), D_MODEL ** -0.5)
    router_b = nrm(ks[17], (DEPTH, N_EXPERTS), 0.01)
    w_up = nrm(ks[18], (DEPTH, N_EXPERTS, D_MODEL, 2 * D_FF), D_MODEL ** -0.5)
    b_up = nrm(ks[19], (DEPTH, N_EXPERTS, 2 * D_FF), 0.01)
    w_down = nrm(ks[20], (DEPTH, N_EXPERTS, D_FF, D_MODEL), D_FF ** -0.5)
    b_down = nrm(ks[21], (DEPTH, N_EXPERTS, D_MODEL), 0.01)
    final_norm_g = 1.0 + nrm(ks[22], (D_MODEL,), 0.05)
    return {"x": x, "meta_tokens": meta_tokens, "mix_norm_g": mix_norm_g, "w_in": w_in,
            "ssm_a_re": ssm_a_re, "ssm_a_im": ssm_a_im, "ssm_log_dt": ssm_log_dt,
            "ssm_b_re": ssm_b_re, "ssm_b_im": ssm_b_im, "ssm_c_re": ssm_c_re, "ssm_c_im": ssm_c_im,
            "ssm_d": ssm_d, "w_ssm_glu": w_ssm_glu, "attn_sinks": attn_sinks, "w_attn_o": w_attn_o,
            "w_out": w_out, "ffn_norm_g": ffn_norm_g, "router_w": router_w, "router_b": router_b,
            "w_up": w_up, "b_up": b_up, "w_down": w_down, "b_down": b_down,
            "final_norm_g": final_norm_g}

def reference(x, meta_tokens, mix_norm_g, w_in, ssm_a_re, ssm_a_im, ssm_log_dt, ssm_b_re, ssm_b_im,
              ssm_c_re, ssm_c_im, ssm_d, w_ssm_glu, attn_sinks, w_attn_o, w_out, ffn_norm_g,
              router_w, router_b, w_up, b_up, w_down, b_down, final_norm_g):
    bsz = x.shape[0]
    meta = jnp.broadcast_to(meta_tokens[None].astype(x.dtype), (bsz, N_META, D_MODEL))
    h = jnp.concatenate([meta, x], axis=1)
    seq_len = h.shape[1]
    splits = [SSM_WIDTH, SSM_WIDTH + Q_WIDTH, SSM_WIDTH + Q_WIDTH + KV_WIDTH,
              SSM_WIDTH + Q_WIDTH + 2 * KV_WIDTH, SSM_WIDTH + Q_WIDTH + 2 * KV_WIDTH + D_MODEL]
    for layer in range(DEPTH):
        hn = rms_norm(h, mix_norm_g[layer])
        proj = hn @ w_in[layer]
        u, q, k, v, g_ssm, g_attn = jnp.split(proj, splits, axis=-1)
        y_ssm = s5_mixer(u, ssm_a_re[layer], ssm_a_im[layer], ssm_log_dt[layer], ssm_b_re[layer],
                         ssm_b_im[layer], ssm_c_re[layer], ssm_c_im[layer], ssm_d[layer])
        glu = jax.nn.gelu(y_ssm) @ w_ssm_glu[layer]
        branch_ssm = glu[..., :D_MODEL] * jax.nn.sigmoid(glu[..., D_MODEL:])
        attn = window_attention(q.reshape(bsz, seq_len, N_HEADS, HEAD_DIM),
                                k.reshape(bsz, seq_len, N_KV_HEADS, HEAD_DIM),
                                v.reshape(bsz, seq_len, N_KV_HEADS, HEAD_DIM),
                                attn_sinks[layer])
        branch_attn = attn @ w_attn_o[layer]
        merged = jax.nn.sigmoid(g_ssm) * branch_ssm + jax.nn.sigmoid(g_attn) * branch_attn
        h = h + merged @ w_out[layer]
        hf = rms_norm(h, ffn_norm_g[layer]).reshape(bsz * seq_len, D_MODEL)
        h = h + moe_ffn(hf, router_w[layer], router_b[layer], w_up[layer], b_up[layer],
                        w_down[layer], b_down[layer]).reshape(bsz, seq_len, D_MODEL)
    h = rms_norm(h, final_norm_g)
    return h[:, N_META:]


_drawn_inputs = setup_inputs


def setup_inputs(seed=0):
    import zlib

    import numpy as np

    out = dict(_drawn_inputs(seed))
    spreads = {}
    factors = {'ssm_a_re': 200.0,
     'attn_sinks': 7.991,
     'b_up': 8.0,
     'b_down': 8.0,
     'ssm_log_dt': 22.56,
     'ssm_b_re': 22.512,
     'ssm_a_im': 8.0,
     'ssm_b_im': 8.0,
     'ssm_c_re': 8.0,
     'ssm_c_im': 8.0}
    for name, (base, spread) in spreads.items():
        noise = np.random.default_rng([zlib.crc32(name.encode()), seed]).standard_normal(out[name].shape)
        drawn = base * np.exp(spread * noise) if base else spread * noise
        out[name] = jnp.asarray(drawn.astype(out[name].dtype))
    for name, factor in factors.items():
        out[name] = (out[name] * factor).astype(out[name].dtype)
    return out
```

```python
import math
from contextlib import ExitStack

import concourse.bass as bass
from concourse import mybir

P = 128
F32 = mybir.dt.float32
F32R = mybir.dt.float32r
I32 = mybir.dt.int32
U32 = mybir.dt.uint32
ALU = mybir.AluOpType
ACT = mybir.ActivationFunctionType
AX_X = mybir.AxisListType.X

D = 1024
SEQ = 1024
META = 16
LEN = SEQ + META
KT = D // P
NTOK = SEQ // P
SSM_W = 512
G = 32
GC = 16
NS = 64
STEP = 8
NCH = LEN // STEP
MCH = META // STEP
OCH = NCH - MCH
HEADS = 16
HD = 64
REP = 8
E_N = 32
FF = 1024
EPS = 1e-5
LIMIT = 7.0
ALPHA = 1.702
HIDE = 1e30

CH = 256
RING = 4
CHW = KT * CH

PASS = 192
PB = PASS - P
REGION = PASS * (-(-SEQ // PASS))
NOVER = (4 * SEQ) // PASS + 1
OVER_PAIRS = (NOVER + 1) // 2
NI = REGION // PASS - 1
UP_CH = 8
DN_CH = 4

TWO_PI_HI = 6.28125
TWO_PI_LO = 2 * math.pi - 6.28125
MAGIC = 1.5 * 2.0 ** 23
SPLIT = 1.5 * 2.0 ** 13


class Tally:

    def __init__(self, sem):
        self.sem, self.n, self.trip, self.per = sem, 0, None, 0

    def mark(self, ins, by=1):
        ins.then_inc(self.sem, by)
        self.n += by

    def now(self):
        return self.n if self.trip is None else self.trip * self.per + self.n

    def enter(self, trip, per):
        self.trip, self.per, self.start = trip, per, self.n

    def leave(self, trips):
        assert self.n - self.start == self.per, (self.n - self.start, self.per)
        self.n = self.start + self.per * trips
        self.trip = None


class Words:

    def __init__(self, t, size):
        self.t, self.size, self.at = t, size, 0

    def take(self, *shape, at=None, parts=P):
        n = math.prod(shape)
        a = self.at if at is None else at
        if at is None:
            self.at += n
        assert a + n <= self.size, (a, n, self.size)
        v = self.t[0:parts, a:a + n]
        if len(shape) == 2:
            v = v.rearrange("p (a b) -> p a b", b=shape[1])
        elif len(shape) == 3:
            v = v.rearrange("p (a b c) -> p a b c", b=shape[1], c=shape[2])
        return v


def bc(ap, axis, n):
    v = ap.unsqueeze(axis)
    return v.broadcast_to(list(v.shape[:axis]) + [n] + list(v.shape[axis + 1:]))


def build_trunk(nc, x, meta_tokens, mix_norm_g, w_in, ssm_a_re, ssm_a_im, ssm_log_dt, ssm_b_re, ssm_b_im,
                ssm_c_re, ssm_c_im, ssm_d, w_ssm_glu, attn_sinks, w_attn_o, w_out, ffn_norm_g,
                router_w, router_b, w_up, b_up, w_down, b_down, final_norm_g, out):
    x_rows = x.rearrange("b s d -> (b s) d")
    out_rows = out.rearrange("b s d -> (b s) d")

    def cols(w, c, n=CH):
        return w.rearrange("l (k p) f -> p (l k) f", p=P)[:, :, c:c + n]

    U0, Q0, K0, GS0, GA0 = 0, SSM_W, SSM_W + D, SSM_W + D + 256, SSM_W + D + 256 + D

    def std(s):
        return ring[:, s * CHW:(s + 1) * CHW].rearrange("p (k f) -> p k f", f=CH)

    def glu_view(s):
        return ring[:, s * CHW:(s + 1) * CHW].rearrange("p (h k f) -> p h k f", h=2, f=CH)

    chunk_of = {}
    chunks = []

    def add_chunk(name, *src):
        chunk_of[name] = len(chunks)
        chunks.append(src)

    for c in range(2):
        add_chunk(("u", c), cols(w_in, U0 + c * CH))
    add_chunk("kv", cols(w_in, K0))
    for c in range(4):
        add_chunk(("q", c), cols(w_in, Q0 + c * CH))
    for c in range(4):
        add_chunk(("gs", c), cols(w_in, GS0 + c * CH))
        add_chunk(("glu", c), cols(w_ssm_glu, c * CH), cols(w_ssm_glu, D + c * CH))
        add_chunk(("ga", c), cols(w_in, GA0 + c * CH))
        add_chunk(("ao", c), cols(w_attn_o, c * CH))
    for c in range(4):
        add_chunk(("out", c), cols(w_out, c * CH))
    NPRE = len(chunks)
    names = {n: name for name, n in chunk_of.items()}

    with ExitStack() as ctx:
        def sem(name):
            return ctx.enter_context(nc.semaphore(name))

        def sems(name, n):
            return [sem(f"{name}{i}") for i in range(n)]

        bank = [ctx.enter_context(nc.psum_tensor(f"bank{i}", [P, 512], F32)) for i in range(8)]
        ring = ctx.enter_context(nc.sbuf_tensor("ring", [P, RING * CHW], F32))
        ring = ring[:, :]

        NCONST = 1800
        const_t = ctx.enter_context(nc.sbuf_tensor("consts", [P, NCONST], F32))
        cw = Words(const_t, NCONST)
        ident = cw.take(P)
        turn = cw.take(2 * P)
        hide = cw.take(META + 2 * P)
        before = cw.take(P)
        ones = cw.take(P)
        step_j = cw.take(NCH)
        step_t = cw.take(2 * STEP)
        sgn = cw.take(1)
        nsgn = cw.take(1)
        half_pi = cw.take(1)
        zero1 = cw.take(1)
        spare = cw.take(2)
        mix_g = cw.take(KT)
        sinks = cw.take(HEADS)
        nsinks = cw.take(HEADS)
        ss = cw.take(NTOK + 1)
        rstd = cw.take(NTOK + 1)
        nw1 = cw.take(NTOK + 1)
        nw2 = cw.take(NTOK + 1)
        ints = cw.take(64)

        NARENA = 43200
        arena_ctx = ExitStack()
        arena_t = arena_ctx.enter_context(nc.sbuf_tensor("arena", [P, NARENA], F32))
        ar = Words(arena_t, NARENA)
        hn_T = ar.take(KT, LEN)
        b_at = ar.at
        q_T = ar.take(KT, SEQ)
        u_at = ar.at
        U = ar.take(G, NCH)
        k_T = [ar.take(META + P + SEQ) for _ in range(2)]
        v_rows = ar.take(NTOK + 1, P)
        v_meta = ar.take(P)
        free_at = ar.at
        u_T = [ar.take(STEP, NCH) for _ in range(2)]
        y_T = ar.take(4, STEP, OCH, at=free_at)[:, :, :, :]
        ar.at = free_at + max(2 * STEP * NCH, 4 * STEP * OCH)
        Ysb = ar.take(8, OCH)
        a_re, a_im, dt_, zz, thr, hi1, lo1, hi8, lo8, skip_d = (ar.take(G) for _ in range(10))
        c1, c2, c3, c4 = (ar.take(G) for _ in range(4))
        ab_re = ar.take(G, 2 * STEP)
        ab_im = ar.take(G, 2 * STEP)
        B1, B2 = ar.take(G, GC), ar.take(G, GC)
        K1, K2 = ar.take(G, GC), ar.take(G, GC)
        par_at = ar.at
        raw_b1, raw_b2 = ar.take(G, GC), ar.take(G, GC)
        raw_c1, raw_c2 = ar.take(4, P), ar.take(4, P)
        raw_ar, raw_ai = ar.take(P, parts=G), ar.take(P, parts=G)
        raw_d = ar.take(STEP, GC, parts=G)
        raw_dt = ar.take(G)
        ph = [ar.take(G, 2 * STEP) for _ in range(5)]
        BG = 4
        NB = G // BG
        ar.at = par_at
        Cj, Sj, Pa, Pk, Pr = (ar.take(BG, NCH) for _ in range(5))
        decay, Wj, Vj = (ar.take(BG, NCH) for _ in range(3))
        Pj, Qj = ar.take(BG, OCH), ar.take(BG, OCH)
        Wrev = ar.take(BG, 2 * STEP - 1, GC)
        Wtmp = ar.take(BG, STEP, GC)
        ET = ar.take(BG, 3 * P)
        G1, G2, Gtmp = (ar.take(BG, STEP, GC) for _ in range(3))
        x_in = [ar.take(D, at=b_at + t * D) for t in range(NTOK)]
        x_meta = ar.take(D, at=u_at, parts=META)
        junk = ar.take(D, at=u_at + D)
        gy_T = ar.take(4, SEQ, at=u_at)
        ar.at = free_at
        q_blk = [ar.take(HEADS, P) for _ in range(2)]
        s_sb = [ar.take(META + 2 * P) for _ in range(2)]
        p_sb = [ar.take(META + 2 * P) for _ in range(2)]
        pt_sb = [ar.take(3 * P) for _ in range(2)]
        o_sb = [ar.take(HEADS, HD) for _ in range(2)]
        nmax = [ar.take(HEADS) for _ in range(2)]
        rsum = [ar.take(HEADS) for _ in range(2)]
        esink = [ar.take(HEADS) for _ in range(2)]
        rden = [ar.take(HEADS) for _ in range(2)]
        ar.at = free_at
        m_T = ar.take(KT, SEQ)
        sg_s, sg_b, sg_a, m_tmp = (ar.take(4, 512) for _ in range(4))
        u_dram = nc.dram_tensor("u_dram", (4, P, STEP, NCH), F32).ap()
        y_dram = nc.dram_tensor("y_dram", (4, P, STEP, OCH), F32).ap()
        arena_ctx.close()
        ring_landed = sems("ring_landed", RING)
        par_landed = sem("par_landed")
        g_landed = sem("g_landed")
        x_landed = sems("x_landed", NTOK + 1)
        consts_done = sem("consts_done")
        pool_step = Tally(sem("pool_step"))
        dve_step = Tally(sem("dve_step"))
        squares_done = sem("squares_done")
        var_done = sem("var_done")
        root_done = sem("root_done")
        hn_rows_done = sem("hn_rows_done")
        pre_ready = sem("pre_ready")
        pre_drained = sems("pre_drained", 4)
        par_turned = sem("par_turned")
        dt_done = sem("dt_done")
        pow_ready = sem("pow_ready")
        pow_done = sem("pow_done")
        par_done = sem("par_done")
        ang_ready = sem("ang_ready")
        cs_done = sem("cs_done")
        abs_done = sem("abs_done")
        g_done = sem("g_done")
        w_done = sem("w_done")
        et_ready = sem("et_ready")
        et_drained = sem("et_drained")
        xs_ready = sem("xs_ready")
        xs_drained = sem("xs_drained")
        pq_done = sem("pq_done")
        y_ready = sem("y_ready")
        y_drained = sem("y_drained")
        u_out = sems("u_out", 4)
        u_moved = sems("u_moved", 4)
        y_out = sems("y_out", 4)
        y_moved = sems("y_moved", 4)
        gelu_done = sem("gelu_done")
        q_staged = sem("q_staged")
        s_ready = sem("s_ready")
        s_done = sem("s_done")
        p_done = sem("p_done")
        pt_turned = sem("pt_turned")
        pt_a = sem("pt_a")
        pt_b = sem("pt_b")
        pt_used = sem("pt_used")
        o_rows = sem("o_rows")
        sink_in = sem("sink_in")
        sink_out = sem("sink_out")
        at_ready = sem("at_ready")
        at_free = sem("at_free")
        mix_ready = sem("mix_ready")
        h_ready = sem("h_ready")
        mix_drained = sems("mix_drained", 8)
        sig_done = sem("sig_done")
        merged = sem("merged")

        def chunks_of_slot(n):
            return [s for m in range(n % RING, n + 1, RING) for s in chunks[m]]

        def used_when(n):
            name = names[n]
            if name == "kv":
                return pre_ready, NKV
            kind, c = name
            return {"u": (pre_ready, NXT + 6 * (c + 1)), "q": (pre_ready, NKV + 4 * (c + 1)),
                    "gs": (mix_ready, 20 * c + 4), "glu": (mix_ready, 20 * c + 12),
                    "ga": (mix_ready, 20 * c + 16), "ao": (mix_ready, 20 * c + 20),
                    "out": (h_ready, 2 * NTOK)}[kind]

        def slot(name):
            return std(chunk_of[name] % RING)

        def pre_bank(r):
            return bank[4 + r % 4]

        NXT = 2 * NTOK + 1
        PIECES = [(0, 352), (352, 344), (696, 344)]
        NU = NXT + 4 * len(PIECES)
        NKV = NU + 6

        def act_attention(act):
            act.wait_ge(gelu_done, 4)
            act.sem_inc(p_done, 2)
            act.sem_inc(pt_b, 2)
            act.sem_inc(at_free, 2)
            with act.Fori(0, NTOK // 2) as it:
                for i in range(32 + 4):
                    if i < 32:
                        half, h = divmod(i, HEADS)
                        act.wait_ge(s_done, it * 32 + i + 1 + 2)
                        act.wait_ge(pt_turned, it * 32 + i + 1)
                        act.activation(p_sb[i % 2], s_sb[i % 2], ACT.Exp, bias=nmax[half][:, h:h + 1], scale=-1.0,
                                       accum_out=rsum[half][:, h:h + 1]).then_inc(p_done, 1)
                    if 2 <= i < 34:
                        j = i - 2
                        act.wait_ge(pt_a, it * 32 + j + 1 + 2)
                        act.wait_ge(pt_used, it * 32 + j + 1)
                        act.activation(pt_sb[j % 2][0:META, 2 * P:3 * P], bank[2 + j % 2][0:META, 2 * P:3 * P], ACT.Copy)\
                           .then_inc(pt_b, 1)
                    if i % 8 == 2 and i > 8:
                        q8 = i // 8 - 1
                        half, hs = q8 // 2, slice((q8 % 2) * 8, (q8 % 2) * 8 + 8)
                        act.wait_ge(sink_in, it * 4 + q8 + 1)
                        act.activation(esink[half][:, hs], esink[half][:, hs], ACT.Exp).then_inc(sink_out, 1)
                    if i == 26:
                        turned(act, it, 0)
                turned(act, it, 1)

        def turned(act, it, half):
            for c in range(2):
                act.wait_ge(at_ready, it * 4 + half * 2 + c + 1 + 4)
                act.activation(q_T[:, 4 * c:4 * c + 4, bass.ds((it * 2 + half) * P, P)],
                               bank[6 + c][:, :].rearrange("p (a b) -> p a b", b=P), ACT.Copy).then_inc(at_free, 1)

        def act_merge(act):
            for c in range(4):
                for kind, dst in ((0, sg_s), (1, sg_b), (3, sg_a)):
                    for g in range(4):
                        u = c * 20 + kind * 4 + g
                        act.wait_ge(mix_ready, u + 1)
                        if c >= 1 and kind in (0, 1) and g == 0:
                            v = (c - 1) * 20 + 11
                            act.wait_ge(mix_drained[v % 8], v // 8 + 1)
                        if c >= 1 and kind == 3 and g == 0:
                            act.wait_ge(merged, 4 * c)
                        act.activation(dst[:, g, :], bank[u % 8][:, :], ACT.Sigmoid).then_inc(mix_drained[u % 8], 1)

        def newton(dve, link, r, v, tmp):
            link(dve.tensor_tensor(tmp, r, r, ALU.mult))
            link(dve.tensor_tensor(tmp, tmp, v, ALU.mult))
            link(dve.tensor_scalar(tmp, tmp, -0.5, 1.5, ALU.mult, ALU.add))
            link(dve.tensor_tensor(r, r, tmp, ALU.mult))

        def dve_attention(dve, step, link):
            dve.wait_ge(gelu_done, 4)
            dve.sem_inc(s_done, 2)
            dve.sem_inc(pt_a, 2)
            dve.sem_inc(o_rows, 2)
            with dve.Fori(0, NTOK // 2) as it:
                step.enter(it, 8)
                for i in range(32 + 5):
                    if i < 32:
                        half, h = divmod(i, HEADS)
                        dve.wait_ge(s_ready, it * 32 + i + 1 + 32)
                        dve.wait_ge(p_done, it * 32 + i + 1)
                    if i < 2:
                        dve.memset(spare[:, i:i + 1], 0.0)
                    if 2 <= i < 34:
                        j = i - 2
                        dve.wait_ge(pt_turned, it * 32 + j + 1 + 2)
                        dve.wait_ge(pt_used, it * 32 + j + 1)
                        dve.tensor_copy(pt_sb[j % 2][:, 0:2 * P], bank[2 + j % 2][:, 0:2 * P]).then_inc(pt_a, 1)
                    if i < 32:
                        dve.tensor_tensor_reduce(s_sb[i % 2], bank[i % 2][:, 0:2 * P + META], hide, 1.0,
                                                 nsinks[:, h:h + 1], ALU.add, ALU.min, nmax[half][:, h:h + 1]).then_inc(s_done, 1)
                    if i % 8 == 1 and i > 8:
                        q8 = i // 8 - 1
                        half, hs = q8 // 2, slice((q8 % 2) * 8, (q8 % 2) * 8 + 8)
                        dve.wait_ge(s_done, it * 32 + 8 * q8 + 8 + 2)
                        dve.tensor_tensor(esink[half][:, hs], nmax[half][:, hs], sinks[:, hs], ALU.add).then_inc(sink_in, 1)
                    if i % 8 == 4 and i > 8:
                        q8 = i // 8 - 1
                        half, hs = q8 // 2, slice((q8 % 2) * 8, (q8 % 2) * 8 + 8)
                        dve.wait_ge(sink_out, it * 4 + q8 + 1)
                        dve.wait_ge(pt_used, it * 32 + 8 * q8 + 8 + 2)
                        link(dve.tensor_tensor(rden[half][:, hs], esink[half][:, hs], rsum[half][:, hs], ALU.add))
                        link(dve.reciprocal(rden[half][:, hs], rden[half][:, hs]))
                        dve.wait_ge(at_ready, it * 4 + half * 2 + 2)
                        dve.tensor_tensor(o_sb[half][:, hs, :], bank[4 + q8 % 2][:, :].rearrange("p (h d) -> p h d", d=HD),
                                          bc(rden[half][:, hs], 2, HD), ALU.mult).then_inc(o_rows, 1)
                step.leave(NTOK // 2)

        def dve_merge(dve, step):
            def drained(u):
                dve.wait_ge(mix_drained[u % 8], u // 8 + 1)

            dve.wait_ge(at_free, 2 * NTOK + 2)
            for c in range(4):
                drained(c * 20 + 7)
                step.mark(dve.tensor_tensor(sg_b, sg_b, sg_s, ALU.mult))
                dve.wait_ge(step.sem, step.now())
                for g in range(4):
                    u = c * 20 + 8 + g
                    dve.wait_ge(mix_ready, u + 1)
                    m = m_T[:, 2 * c + g // 2, (g % 2) * 512:(g % 2 + 1) * 512]
                    dve.tensor_tensor(m, bank[u % 8][:, :], sg_b[:, g, :], ALU.mult).then_inc(mix_drained[u % 8], 1)
                for g in range(4):
                    u = c * 20 + 16 + g
                    m = m_T[:, 2 * c + g // 2, (g % 2) * 512:(g % 2 + 1) * 512]
                    drained(c * 20 + 12 + g)
                    dve.wait_ge(mix_ready, u + 1)
                    dve.tensor_tensor(m_tmp[:, g, :], bank[u % 8][:, :], sg_a[:, g, :], ALU.mult).then_inc(mix_drained[u % 8], 1)
                    drained(u)
                    dve.tensor_tensor(m, m, m_tmp[:, g, :], ALU.add).then_inc(merged, 1)

        rw_ = Words(arena_t, NARENA)
        h_rows = rw_.take(NTOK, D)
        hf_rows = [rw_.take(D) for _ in range(2)]
        hf_T = [rw_.take(KT, P) for _ in range(2)]
        ffn_g = rw_.take(D)
        h_junk = rw_.take(D)
        bdown = rw_.take(D, parts=E_N)
        assert rw_.at <= free_at
        SMALL = free_at + KT * SEQ
        rs = Words(arena_t, NARENA)
        rs.at = SMALL
        rout_w = rs.take(KT, E_N)
        rout_b = rs.take(E_N)
        h_ss, h_r, h_v, h_t = (rs.take(NTOK) for _ in range(4))
        logit = rs.take(NTOK, E_N)
        top_v = rs.take(NTOK, 8)
        top_e = rs.take(NTOK, 4)
        top_i = rs.take(NTOK * 8).bitcast(U32).rearrange("p (t k) -> p t k", k=8)
        expo, esum = rs.take(NTOK, 4), rs.take(NTOK)
        ntop = rs.take(NTOK)
        gate = rs.take(NTOK, 4)
        pick = rs.take(2, 4, E_N)
        pick_g = rs.take(4, E_N)
        pick_s = rs.take(4, E_N)
        picked = rs.take(NTOK, E_N)
        running = rs.take(NTOK + 1, E_N)
        gmat = rs.take(NTOK, E_N)
        gmat_T = rs.take(2, P, parts=E_N)
        place = rs.take(NTOK, E_N)
        slot_f = rs.take(NTOK, 4)
        e_iota, e_region = rs.take(E_N), rs.take(E_N)
        entry = rs.take(NTOK * 16)
        slot_i = rs.take(NTOK * 4).bitcast(I32)
        FILL = 96
        empty = rs.take(4 * FILL).bitcast(I32).rearrange("p (r f) -> p r f", f=4)
        NF = E_N * NI
        flag, cum, sel_q, base_f, exp_f, ones_f = (rs.take(NF) for _ in range(6))
        over_q = rs.take(1)
        over_v = rs.take(4)
        over_vi = rs.take(4).bitcast(I32)
        count_b = rs.take(E_N)
        over_row = rs.take(4 * P, parts=1).bitcast(I32)
        raw_bias = rs.take(4, P)
        bias_T = rs.take(E_N * 16)
        bias_now = [rs.take(16) for _ in range(2)]
        final_g = rs.take(D)
        entry_i = entry.bitcast(I32).rearrange("p (t k f) -> p t k f", k=4, f=4)
        entry_f = entry.rearrange("p (t k f) -> p t k f", k=4, f=4)

        ew = Words(arena_t, NARENA)
        x_T = [ew.take(KT, PASS) for _ in range(2)]
        a_T = ew.take(KT, PASS)
        gat = [[ew.take(D), ew.take(D, parts=PB)] for _ in range(2)]
        y_sb = [[ew.take(D), ew.take(D, parts=PB)] for _ in range(2)]
        glu_s = [ew.take(2, PASS) for _ in range(2)]
        lin_s = [ew.take(2, PASS) for _ in range(2)]
        sig_s = [ew.take(2, PASS) for _ in range(2)]
        idx = [[ew.take(4).bitcast(I32), ew.take(4, parts=PB).bitcast(I32)] for _ in range(2)]
        assert ew.at <= SMALL
        FB = 3
        fw = Words(arena_t, NARENA)
        fin = [fw.take(5, D) for _ in range(FB)]
        fin_junk = fw.take(D)
        fin_ss, fin_r, fin_v, fin_t = (fw.take(NTOK) for _ in range(4))
        assert fw.at <= SMALL

        NPASS = E_N + NOVER
        NSLOT = E_N * REGION
        hf_dram = nc.dram_tensor("hf_dram", (SEQ, D), F32).ap()
        h_dram = nc.dram_tensor("h_dram", (SEQ, D), F32).ap()
        y_rows_dram = nc.dram_tensor("y_rows_dram", (4 * SEQ, D), F32).ap()
        table = nc.dram_tensor("table", (NSLOT, 4), I32).ap()
        over_dram = nc.dram_tensor("over_dram", (P, 4), I32).ap()

        r_loads = sem("r_loads")
        xa_landed = sems("xa_landed", NTOK)
        h_added = sem("h_added")
        sq_done = sem("sq_done")
        v_done = sem("v_done")
        rt_done = sem("rt_done")
        hf_done = sem("hf_done")
        hf_stored = sems("hf_stored", 2)
        hf_turned = sem("hf_turned")
        hf_T_done = sem("hf_T_done")
        logits_ready = sem("logits_ready")
        exp_in = sem("exp_in")
        exp_out = sem("exp_out")
        picked_done = sem("picked_done")
        pos_ready = sem("pos_ready")
        place_done = sem("place_done")
        slot_done = sem("slot_done")
        bias_ready = sem("bias_ready")
        h2_added = sem("h2_added")
        h2_stored = sem("h2_stored")
        rc_done = sem("rc_done")
        filled = sem("filled")
        entered = sem("entered")
        bup_turned = sem("bup_turned")
        bup_done = sem("bup_done")
        counts_ready = sem("counts_ready")
        over_done = sem("over_done")
        over_out = sem("over_out")
        over_in = sem("over_in")
        ids_landed = sem("ids_landed")
        pool_passed = sem("pool_passed")
        gathered = sems("gathered", 2)
        scattered = sem("scattered")
        x_turned = sem("x_turned")
        x_stored = sem("x_stored")
        up_drained = sem("up_drained")
        sigm_done = sem("sigm_done")
        a_done = sem("a_done")
        y_done = sem("y_done")
        given = sem("given")
        pe_done = sem("pe_done")
        bias_sem = sem("bias_sem")
        fin_step = sem("fin_step")
        experts_done = sem("experts_done")
        fin_landed = sems("fin_landed", FB)
        fg_landed = sem("fg_landed")
        fin_sum = sem("fin_sum")
        fin_sq = sem("fin_sq")
        fin_var = sem("fin_var")
        fin_root = sem("fin_root")
        fin_done = sem("fin_done")
        stored = sems("stored", FB)

        row1 = lambda a: a.partition_broadcast(P).rearrange("p l d -> p (l d)")
        w_up_v = w_up.rearrange("l e (k p) f -> p (l e) k f", p=P)
        w_dn_v = w_down.rearrange("l e (k p) f -> p (l e) k f", p=P)

        def chunk_src(e, c):
            v, f = (w_up_v, (c % 2) * FF + (c // 2) * CH) if c < UP_CH else (w_dn_v, (c - UP_CH) * CH)
            return v[:, bass.ds(e, 1), :, f:f + CH].rearrange("p e k f -> p (e k) f")

        def experts_sync(sp):
            sp.wait_ge(mix_ready, 80)
            for t in range(NTOK):
                sp.dma_start(h_rows[:, t, :], x_rows[t * P:(t + 1) * P, :]).then_inc(xa_landed[t], 16)
            sp.dma_start(ffn_g, row1(ffn_norm_g)).then_inc(r_loads, 16)
            sp.dma_start(bdown, b_down.rearrange("l e d -> (l e) d")).then_inc(r_loads, 16)
            sp.wait_ge(merged, 16)
            sp.dma_start(rout_w, router_w.rearrange("l (k p) e -> p (l k) e", p=P)).then_inc(r_loads, 16)
            sp.dma_start(rout_b, row1(router_b)).then_inc(r_loads, 16)
            sp.dma_start(raw_bias, b_up.rearrange("l (a e) (t p) -> (e t) (l a) p", a=4, p=P)).then_inc(r_loads, 16)
            sp.dma_start(final_g, final_norm_g.partition_broadcast(P)).then_inc(fg_landed, 16)

            def pass_weights(e, p):
                for c in range(UP_CH + DN_CH):
                    sp.wait_ge(pe_done, p * 12 + c + 1)
                    s = (NPRE + c) % RING
                    sp.dma_start(std(s), chunk_src(e, c)).then_inc(ring_landed[s], 16)

            sp.wait_ge(h_ready, 2 * NTOK)
            with sp.Fori(0, E_N) as p:
                pass_weights(p, p)
            sp.wait_ge(over_in, 16)
            n = sp.value_load(over_row[0:1, 2:3], min_val=0, max_val=NOVER)
            with sp.Fori(0, NOVER) as q:
                with sp.If(q < n):
                    e = sp.value_load(over_row[0:1, bass.ds(q * 4 + 1, 1)], min_val=0, max_val=E_N - 1)
                    pass_weights(e, q + E_N)
            sp.wait_ge(experts_done, 1)
            for t in range(NTOK):
                if t >= FB:
                    sp.wait_ge(fin_sum, t - FB + 1)
                    sp.wait_ge(stored[t % FB], 16 * (t // FB))
                b = fin[t % FB]
                sp.dma_start(b[:, 0, :], h_dram[t * P:(t + 1) * P, :]).then_inc(fin_landed[t % FB], 16)
                sp.dma_start(b[:, 1:5, :], y_rows_dram.rearrange("(k r) d -> r k d", k=4)[t * P:(t + 1) * P]).then_inc(fin_landed[t % FB], 16)
            for b in range(FB):
                sp.wait_ge(stored[b], 16 * len(range(b, NTOK, FB)))

        def experts_pool(pool):
            cn = [0]

            def const(ins):
                ins.then_inc(rc_done, 1)
                cn[0] += 1
                pool.wait_ge(rc_done, cn[0])

            pool.wait_ge(merged, 16)
            const(pool.iota(e_iota, [[1, E_N]], 0, 0, allow_small_or_imprecise_dtypes=True))
            const(pool.iota(e_region, [[REGION, E_N]], 0, 0, allow_small_or_imprecise_dtypes=True))
            const(pool.memset(running[:, 0, :], 0.0))
            const(pool.memset(entry_i[:, :, :, 3], 0))
            const(pool.iota(entry_i[:, :, :, 0], [[P, NTOK], [0, 4]], 0, 1))
            const(pool.iota(entry_i[:, :, :, 1], [[P, NTOK], [SEQ, 4]], 0, 1))
            const(pool.memset(empty, 0))
            const(pool.memset(empty[:, :, 1], 1 << 20))
            const(pool.memset(ones_f, 1.0))
            const(pool.iota(over_q, [[0, 1]], 1, 1, allow_small_or_imprecise_dtypes=True))
            const(pool.iota(exp_f.rearrange("p (i e) -> p i e", e=E_N), [[0, NI], [1, E_N]], 0, 0, allow_small_or_imprecise_dtypes=True))
            const(pool.iota(base_f.rearrange("p (i e) -> p i e", e=E_N), [[PASS, NI], [REGION, E_N]], PASS, 0, allow_small_or_imprecise_dtypes=True))
            NFILL = NSLOT // (P * FILL)
            for a in range(NFILL):
                pool.dma_start(table[a * P * FILL:(a + 1) * P * FILL, :].rearrange("(p r) f -> p r f", p=P), empty).then_inc(filled, 16)
            for s in range(NTOK + 4):
                if s < NTOK:
                    pool.wait_ge(hf_done, s + 1)
                    pool.dma_start(hf_dram[s * P:(s + 1) * P, :], hf_rows[s % 2]).then_inc(hf_stored[s % 2], 16)
                if s == 3:
                    pool.wait_ge(filled, 16 * NFILL)
                if s >= 4:
                    t = s - 4
                    pool.wait_ge(h2_added, 2 * t + 2)
                    pool.dma_start(h_dram[t * P:(t + 1) * P, :], h_rows[:, t, :]).then_inc(h2_stored, 16)
                if 3 <= s < NTOK + 3:
                    t = s - 3
                    pool.wait_ge(slot_done, t + 1)
                    for k in range(4):
                        pool.indirect_dma_start(table, bass.IndirectOffsetOnAxis(ap=slot_i[:, 4 * t + k:4 * t + k + 1], axis=0),
                                                entry_i[:, t, k, :], None, bounds_check=NSLOT - 1).then_inc(entered, 16)
            pool.wait_ge(over_done, 1)
            pool.dma_start(over_dram, over_vi).then_inc(over_out, 16)
            pool.wait_ge(over_out, 16)
            pool.dma_start(over_row, over_dram.rearrange("(o q) f -> o (q f)", o=1)).then_inc(over_in, 16)
            for b in range(2):
                pool.wait_ge(hf_stored[b], 16 * NTOK // 2)
            pool.wait_ge(h2_stored, 16 * NTOK)
            pool.wait_ge(entered, 64 * NTOK)
            pool.wait_ge(over_in, 16)
            pool.wait_ge(bup_done, 1)

            def fetch(j, base, p):
                for b, n in ((0, P), (1, PB)):
                    pool.dma_start(idx[j][b], table[bass.ds(base + b * P, n), :]).then_inc(ids_landed, 16)
                pool.wait_ge(ids_landed, p * 32 + 32)
                pool.sem_inc(pool_passed, 1)
                for b, n in ((0, P), (1, PB)):
                    pool.indirect_dma_start(gat[j][b], None, hf_dram, bass.IndirectOffsetOnAxis(ap=idx[j][b][:, 0:1], axis=0),
                                            bounds_check=SEQ - 1).then_inc(gathered[j], 16)

            def give(j, p):
                pool.wait_ge(y_done, p * 2 + 2 + 2)
                pool.sem_inc(pool_passed, 1)
                for b, n in ((0, P), (1, PB)):
                    pool.indirect_dma_start(y_rows_dram, bass.IndirectOffsetOnAxis(ap=idx[j][b][:, 1:2], axis=0),
                                            y_sb[j][b], None, bounds_check=4 * SEQ - 1, oob_is_err=False).then_inc(scattered, 16)

            def fetch_next(j, p):
                pool.wait_ge(scattered, p * 32 + 32)
                pool.wait_ge(x_turned, p * 4 + 4)
                pool.sem_inc(given, 1)
                fetch(j, (p + 2) * REGION, p + 2)

            pool.sem_inc(given, 2)
            fetch(0, 0, 0)
            fetch(1, REGION, 1)
            with pool.Fori(0, E_N // 2 - 1) as h:
                for j in range(2):
                    give(j, h * 2 + j)
                    fetch_next(j, h * 2 + j)
            for j in range(2):
                give(j, E_N - 2 + j)
            pool.wait_ge(scattered, 32 * E_N)
            pool.sem_inc(given, 2)
            n = pool.value_load(over_row[0:1, 2:3], min_val=0, max_val=NOVER)
            with pool.Fori(0, NOVER) as q:
                with pool.If(q < n):
                    base = pool.value_load(over_row[0:1, bass.ds(q * 4, 1)], min_val=0, max_val=NSLOT - PASS)
                    fetch(0, base, q + E_N)
                    give(0, q + E_N)
                    pool.wait_ge(scattered, (q + E_N) * 32 + 32)
                    pool.sem_inc(given, 1)
            pool.wait_ge(scattered, n * 32 + 32 * E_N)
            pool.sem_inc(experts_done, 1)

        def experts_act(act):
            for s in range(NTOK + 3):
                if s < NTOK:
                    t = s
                    act.wait_ge(h_added, 2 * t + 2)
                    if t >= 1:
                        act.wait_ge(sq_done, t)
                    act.activation(h_junk, h_rows[:, t, :], ACT.Square, accum_out=h_ss[:, t:t + 1]).then_inc(sq_done, 1)
                    act.wait_ge(v_done, t + 1)
                    act.activation(h_r[:, t:t + 1], h_v[:, t:t + 1], ACT.Sqrt).then_inc(rt_done, 1)
                if 1 <= s <= NTOK:
                    t = s - 1
                    if t >= 2:
                        act.wait_ge(logits_ready, t - 1)
                    for c in range(2):
                        act.wait_ge(hf_turned, 2 * t + c + 1)
                        act.activation(hf_T[t % 2][:, 4 * c:4 * c + 4, :].rearrange("p a b -> p (a b)"), bank[4 + c][:, :], ACT.Copy)\
                           .then_inc(hf_T_done, 1)
                if 2 <= s < NTOK + 2:
                    t = s - 2
                    act.wait_ge(exp_in, t + 1)
                    act.activation(expo[:, t, :], top_v[:, t, 0:4], ACT.Exp, bias=ntop[:, t:t + 1],
                                   accum_out=esum[:, t:t + 1]).then_inc(exp_out, 1)

            def act_pass(j, p):
                for i in range(4):
                    act.wait_ge(up_drained, p * 8 + 2 * i + 1)
                    act.activation(sig_s[i % 2], glu_s[i % 2], ACT.Sigmoid, scale=ALPHA).then_inc(sigm_done, 1)
                for h in range(2):
                    act.wait_ge(pe_done, p * 12 + UP_CH + 2 * h + 2 + 4)
                    if h == 0:
                        act.wait_ge(given, p + 1)
                    for b, n in ((0, P), (1, PB)):
                        ins = act.activation(y_sb[j][b][:, h * 512:(h + 1) * 512], bank[4 + 2 * b + h][0:n, :], ACT.Copy,
                                             scale=idx[j][b][:, 2:3].bitcast(F32))
                    ins.then_inc(y_done, 1)

            act.sem_inc(y_done, 2)
            with act.Fori(0, E_N // 2) as h:
                for j in range(2):
                    act_pass(j, h * 2 + j)
            n = act.value_load(over_row[0:1, 2:3], min_val=0, max_val=NOVER)
            with act.Fori(0, NOVER) as q:
                with act.If(q < n):
                    act_pass(0, q + E_N)
            for t in range(NTOK):
                act.wait_ge(fin_sum, t + 1)
                if t >= 1:
                    act.wait_ge(fin_sq, t)
                act.activation(fin_junk, fin[t % FB][:, 0, :], ACT.Square, accum_out=fin_ss[:, t:t + 1]).then_inc(fin_sq, 1)
                act.wait_ge(fin_var, t + 1)
                act.activation(fin_r[:, t:t + 1], fin_v[:, t:t + 1], ACT.Sqrt).then_inc(fin_root, 1)
                act.wait_ge(fin_done, t + 1)
                act.dma_start(out_rows[t * P:(t + 1) * P, :], fin[t % FB][:, 0, :]).then_inc(stored[t % FB], 16)

        def experts_dve(dve):
            step = dve_step

            def link(ins):
                step.mark(ins)
                dve.wait_ge(step.sem, step.now())

            dve.wait_ge(mix_ready, 80)
            dve.wait_ge(merged, 16)
            dve.wait_ge(r_loads, 16 * 5)
            dve.wait_ge(rc_done, 12)
            for s in range(NTOK + 4):
                if s < NTOK:
                    t = s
                    dve.wait_ge(xa_landed[t], 16)
                    for c in range(2):
                        dve.wait_ge(h_ready, 2 * t + c + 1)
                        hh = h_rows[:, t, c * 512:(c + 1) * 512]
                        dve.tensor_tensor(hh, hh, bank[2 * (t % 2) + c][:, :], ALU.add).then_inc(h_added, 1)
                    ht = slice(t, t + 1)
                    dve.wait_ge(sq_done, t + 1)
                    dve.tensor_scalar(h_v[:, ht], h_ss[:, ht], 1.0 / D, EPS, ALU.mult, ALU.add).then_inc(v_done, 1)
                    dve.wait_ge(rt_done, t + 1)
                    link(dve.reciprocal(h_r[:, ht], h_r[:, ht]))
                    newton(dve, link, h_r[:, ht], h_v[:, ht], h_t[:, ht])
                    if t >= 2:
                        dve.wait_ge(hf_stored[t % 2], 16 * (t // 2))
                        dve.wait_ge(hf_turned, 2 * (t - 1))
                    dve.scalar_tensor_tensor(hf_rows[t % 2], h_rows[:, t, :], h_r[:, ht], ffn_g, ALU.mult, ALU.mult).then_inc(hf_done, 1)
                if s >= 4:
                    t = s - 4
                    for c in range(2):
                        dve.wait_ge(bias_ready, 2 * t + c + 1)
                        hh = h_rows[:, t, c * 512:(c + 1) * 512]
                        dve.tensor_tensor(hh, hh, bank[4 + c][:, :], ALU.add).then_inc(h2_added, 1)
                if 2 <= s < NTOK + 2:
                    t = s - 2
                    dve.wait_ge(logits_ready, t + 1)
                    link(dve.tensor_tensor(logit[:, t, :], bank[6][:, 0:E_N], rout_b, ALU.add))
                    link(dve.max(top_v[:, t, :], logit[:, t, :]))
                    dve.tensor_scalar(ntop[:, t:t + 1], top_v[:, t, 0:1], -1.0, None, ALU.mult).then_inc(exp_in, 1)
                    link(dve.max_index(top_i[:, t, :], top_v[:, t, :], logit[:, t, :]))
                    link(dve.tensor_copy(top_e[:, t, :], top_i[:, t, 0:4]))
                    if t >= 2:
                        dve.wait_ge(slot_done, t - 1)
                    link(dve.tensor_tensor(pick[:, t % 2], bc(e_iota, 1, 4), bc(top_e[:, t, :], 2, E_N), ALU.is_equal))
                    link(dve.tensor_reduce(picked[:, t, :], pick[:, t % 2].rearrange("p k e -> p e k"), AX_X, ALU.add))
                    link(dve.tensor_tensor(running[:, t + 1, :], running[:, t, :], picked[:, t, :], ALU.add))
                    dve.wait_ge(exp_out, t + 1)
                    link(dve.reciprocal(esum[:, t:t + 1], esum[:, t:t + 1]))
                    link(dve.tensor_scalar(gate[:, t, :], expo[:, t, :], esum[:, t:t + 1], None, ALU.mult))
                    link(dve.tensor_copy(entry_f[:, t, :, 2], gate[:, t, :]))
                    link(dve.tensor_tensor(pick_g, pick[:, t % 2], bc(gate[:, t, :], 2, E_N), ALU.mult))
                    dve.tensor_reduce(gmat[:, t, :], pick_g.rearrange("p k e -> p e k"), AX_X, ALU.add).then_inc(picked_done, 1)
                if 3 <= s < NTOK + 3:
                    t = s - 3
                    dve.wait_ge(pos_ready, t + 1)
                    link(dve.tensor_tensor(place[:, t, :], bank[7][:, 0:E_N], e_region, ALU.add))
                    if t >= 2:
                        dve.wait_ge(bias_ready, 2 * t - 2)
                    dve.tensor_copy(gmat_T[:, t % 2, :], bank[7][0:E_N, P:2 * P]).then_inc(place_done, 1)
                    link(dve.tensor_tensor(pick_s, pick[:, t % 2], bc(place[:, t, :], 1, 4), ALU.mult))
                    link(dve.tensor_reduce(slot_f[:, t, :], pick_s, AX_X, ALU.add))
                    dve.tensor_copy(slot_i[:, 4 * t:4 * t + 4], slot_f[:, t, :]).then_inc(slot_done, 1)
            dve.wait_ge(counts_ready, 1)
            link(dve.tensor_copy(count_b, bank[6][:, 0:E_N]))
            for i in range(NI):
                step.mark(dve.tensor_scalar(flag[:, i * E_N:(i + 1) * E_N], count_b, float(PASS * (i + 1)), None, ALU.is_gt))
            dve.wait_ge(step.sem, step.now())
            link(dve.tensor_tensor_scan(cum, ones_f, flag, 0.0, ALU.mult, ALU.add))
            link(dve.tensor_scalar(sel_q, cum, over_q, None, ALU.is_equal))
            link(dve.tensor_tensor(sel_q, sel_q, flag, ALU.mult))
            link(dve.tensor_tensor(base_f, sel_q, base_f, ALU.mult))
            link(dve.tensor_tensor(exp_f, sel_q, exp_f, ALU.mult))
            link(dve.memset(over_v, 0.0))
            link(dve.tensor_reduce(over_v[:, 0:1], base_f, AX_X, ALU.add))
            link(dve.tensor_reduce(over_v[:, 1:2], exp_f, AX_X, ALU.add))
            link(dve.tensor_copy(over_v[:, 2:3], cum[:, NF - 1:NF]))
            link(dve.tensor_copy(over_v[0:E_N, 3:4], bank[6][0:E_N, E_N:E_N + 1]))
            dve.tensor_copy(over_vi, over_v).then_inc(over_done, 1)
            dve.wait_ge(bup_turned, 1)
            dve.tensor_copy(bias_T, bank[0][:, :]).then_inc(bup_done, 1)
            dve.wait_ge(bup_done, 1)

            def store_x(j, x4):
                for b in range(4):
                    dve.wait_ge(x_turned, x4 + b + 1)
                    dve.tensor_copy(x_T[j][:, 2 * b:2 * b + 2, :].rearrange("p a b -> p (a b)"), bank[b][:, 0:2 * PASS]).then_inc(x_stored, 1)

            def take_bias(j, e):
                dve.tensor_copy(bias_now[j], bias_T[:, bass.ds(e * 16, 16)]).then_inc(bias_sem, 1)

            def dve_pass(j, p, e):
                take_bias(j, e)
                dve.wait_ge(bias_sem, p + 1)
                for i in range(4):
                    v = i % 2
                    dve.wait_ge(a_done, p * 4 + i + 1)
                    for which, dst in ((0, glu_s[v]), (1, lin_s[v])):
                        c = 2 * i + which
                        dve.wait_ge(pe_done, p * 12 + c + 1 + 4)
                        src = bank[c % 4][:, 0:2 * PASS].rearrange("p (a b) -> p a b", b=PASS)
                        for a in range(2):
                            ins = dve.tensor_scalar(dst[:, a, :], src[:, a, :], bias_now[j][:, which * 8 + 2 * i + a:which * 8 + 2 * i + a + 1],
                                                    LIMIT, ALU.add, ALU.min)
                        ins.then_inc(up_drained, 1)
                    dve.wait_ge(up_drained, p * 8 + 2 * i + 2)
                    link(dve.tensor_scalar(lin_s[v], lin_s[v], -LIMIT, 1.0, ALU.max, ALU.add))
                    link(dve.tensor_tensor(lin_s[v], lin_s[v], glu_s[v], ALU.mult))
                    dve.wait_ge(sigm_done, p * 4 + i + 1)
                    dve.tensor_tensor(a_T[:, 2 * i:2 * i + 2, :], lin_s[v], sig_s[v], ALU.mult).then_inc(a_done, 1)

            dve.sem_inc(a_done, 2)
            store_x(0, 0)
            with dve.Fori(0, E_N // 2 - 1) as h:
                step.enter(h, 16)
                for j in range(2):
                    p = h * 2 + j
                    dve_pass(j, p, p)
                    store_x(1 - j, p * 4 + 4)
                step.leave(E_N // 2 - 1)
            dve_pass(0, E_N - 2, E_N - 2)
            store_x(1, 4 * E_N - 4)
            dve_pass(1, E_N - 1, E_N - 1)
            n = dve.value_load(over_row[0:1, 2:3], min_val=0, max_val=NOVER)
            with dve.Fori(0, NOVER) as q:
                with dve.If(q < n):
                    e = dve.value_load(over_row[0:1, bass.ds(q * 4 + 1, 1)], min_val=0, max_val=E_N - 1)
                    store_x(0, q * 4 + 4 * E_N)
                    step.enter(q, 8)
                    dve_pass(0, q + E_N, e)
                    step.trip = None
            fs = Tally(fin_step)

            def flink(ins):
                fs.mark(ins)
                dve.wait_ge(fs.sem, fs.now())

            dve.wait_ge(fg_landed, 16)
            for t in range(NTOK):
                b = fin[t % FB]
                dve.wait_ge(fin_landed[t % FB], 32 * (t // FB + 1))
                flink(dve.tensor_tensor(b[:, 1:3, :], b[:, 1:3, :], b[:, 3:5, :], ALU.add))
                flink(dve.tensor_tensor(b[:, 1, :], b[:, 1, :], b[:, 2, :], ALU.add))
                dve.tensor_tensor(b[:, 0, :], b[:, 0, :], b[:, 1, :], ALU.add).then_inc(fin_sum, 1)
                ft = slice(t, t + 1)
                dve.wait_ge(fin_sq, t + 1)
                dve.tensor_scalar(fin_v[:, ft], fin_ss[:, ft], 1.0 / D, EPS, ALU.mult, ALU.add).then_inc(fin_var, 1)
                dve.wait_ge(fin_root, t + 1)
                flink(dve.reciprocal(fin_r[:, ft], fin_r[:, ft]))
                newton(dve, flink, fin_r[:, ft], fin_v[:, ft], fin_t[:, ft])
                dve.scalar_tensor_tensor(b[:, 0, :], b[:, 0, :], fin_r[:, ft], final_g, ALU.mult, ALU.mult).then_inc(fin_done, 1)

        def experts_pe(pe):
            pe.wait_ge(merged, 16)
            pe.wait_ge(r_loads, 16 * 5)
            for u in range(80 - 8, 80):
                pe.wait_ge(mix_drained[u % 8], u // 8 + 1)
            for s in range(NTOK + 4):
                if s < NTOK:
                    t = s
                    for c in range(4):
                        if t == 0:
                            n = chunk_of[("out", c)]
                            pe.wait_ge(ring_landed[n % RING], 16 * len(chunks_of_slot(n)))
                        if t >= 2 and c % 2 == 0:
                            pe.wait_ge(h_added, 2 * (t - 2) + c // 2 + 1)
                        w = slot(("out", c))
                        for k in range(KT):
                            ins = pe.matmul(bank[2 * (t % 2) + c // 2][:, (c % 2) * CH:(c % 2 + 1) * CH], m_T[:, k, t * P:(t + 1) * P], w[:, k, :],
                                            start=(k == 0), stop=(k == KT - 1))
                        if c % 2:
                            ins.then_inc(h_ready, 1)
                if s >= 4:
                    t = s - 4
                    pe.wait_ge(place_done, t + 1)
                    for c in range(2):
                        pe.wait_ge(hf_T_done, 2 * min(s - 1, NTOK))
                        pe.matmul(bank[4 + c][:, :], gmat_T[:, t % 2, :], bdown[:, c * 512:(c + 1) * 512], start=True, stop=True).then_inc(bias_ready, 1)
                if 2 <= s < NTOK + 2:
                    t = s - 2
                    pe.wait_ge(hf_T_done, 2 * t + 2)
                    if t >= 1:
                        pe.wait_ge(exp_in, t)
                    for k in range(KT):
                        ins = pe.matmul(bank[6][:, 0:E_N], hf_T[t % 2][:, k, :], rout_w[:, k, :], start=(k == 0), stop=(k == KT - 1))
                    ins.then_inc(logits_ready, 1)
                if 3 <= s < NTOK + 3:
                    t = s - 3
                    pe.wait_ge(picked_done, t + 1)
                    if t >= 1:
                        pe.wait_ge(place_done, t)
                    pe.matmul(bank[7][:, 0:E_N], before, picked[:, t, :], start=True, stop=False)
                    pe.matmul(bank[7][:, 0:E_N], ones, running[:, t, :], start=False, stop=True)
                    pe.transpose(bank[7][0:E_N, P:2 * P], gmat[:, t, :], ident).then_inc(pos_ready, 1)
                if 1 <= s <= NTOK:
                    t = s - 1
                    pe.wait_ge(hf_done, t + 1)
                    if t >= 1:
                        pe.wait_ge(hf_T_done, 2 * t)
                    if t >= 3:
                        pe.wait_ge(h2_added, 2 * (t - 3) + 2)
                    for c in range(2):
                        for a in range(4):
                            ins = pe.transpose(bank[4 + c][:, a * P:(a + 1) * P], hf_rows[t % 2][:, (4 * c + a) * P:(4 * c + a + 1) * P], ident)
                        ins.then_inc(hf_turned, 1)
                if s == NTOK + 2:
                    pe.matmul(bank[6][:, 0:E_N], ones, running[:, NTOK, :], start=True, stop=True)
                    pe.matmul(bank[6][0:E_N, E_N:E_N + 1], running[:, NTOK, :], ones[:, 0:1], start=True, stop=True).then_inc(counts_ready, 1)
            pe.wait_ge(h_added, 2 * NTOK)
            for a in range(4):
                ins = pe.transpose(bank[0][:, a * P:(a + 1) * P], raw_bias[:, a, :], ident)
            ins.then_inc(bup_turned, 1)
            pe.wait_ge(bup_done, 1)
            pe.wait_ge(h2_added, 2 * NTOK)
            pe.wait_ge(over_in, 16)

            def turn_x(j, p, uses):
                pe.wait_ge(gathered[j], uses * 32 + 32)
                for b in range(4):
                    if not (isinstance(p, int) and p == 0):
                        pe.wait_ge(up_drained, p * 8 + b - 3)
                    for a in range(2):
                        k = slice((2 * b + a) * P, (2 * b + a + 1) * P)
                        pe.transpose(bank[b][:, a * PASS:a * PASS + P], gat[j][0][:, k], ident)
                        ins = pe.transpose(bank[b][:, a * PASS + P:(a + 1) * PASS], gat[j][1][:, k], ident[0:PB, 0:PB])
                    ins.then_inc(x_turned, 1)

            def landed(p, c):
                s = (NPRE + c) % RING
                base = sum(len(chunks[m]) for m in range(s, NPRE, RING))
                pe.wait_ge(ring_landed[s], p * 48 + 16 * (base + c // RING + 1))
                return std(s)

            def up(j, p, rows):
                for c in range(UP_CH):
                    w = landed(p, c)
                    if c == 0:
                        pe.wait_ge(x_stored, p * 4 + 4)
                    if c >= 4:
                        pe.wait_ge(up_drained, p * 8 + c - 3)
                    for a in range(2):
                        for k in range(KT):
                            ins = pe.matmul(bank[c % 4][:, a * PASS:a * PASS + rows], w[:, k, a * P:(a + 1) * P], x_T[j][:, k, 0:rows],
                                            start=(k == 0), stop=(k == KT - 1))
                    ins.then_inc(pe_done, 1)

            def down(p, rows):
                for c in range(DN_CH):
                    w = landed(p, UP_CH + c)
                    if c % 2 == 0:
                        pe.wait_ge(y_done, p * 2 + c // 2 + 1)
                    for k in range(KT):
                        if c == 0 and k % 2 == 0:
                            pe.wait_ge(a_done, p * 4 + k // 2 + 1 + 2)
                        for b, n in ((0, P), (1, PB))[0:1 if rows <= P else 2]:
                            ins = pe.matmul(bank[4 + 2 * b + c // 2][0:n, (c % 2) * CH:(c % 2 + 1) * CH], a_T[:, k, b * P:b * P + n], w[:, k, :],
                                            start=(k == 0), stop=(k == KT - 1))
                    ins.then_inc(pe_done, 1)

            def pe_pass(j, p, ahead):
                n = pe.value_load(over_row[0:1, bass.ds(p * 4 + 3, 1) if not isinstance(p, int) else slice(4 * p + 3, 4 * p + 4)], min_val=0, max_val=SEQ)
                with pe.If(n < P + 1):
                    up(j, p, P)
                with pe.If(n > P):
                    with pe.If(n < P + 33):
                        up(j, p, P + 32)
                    with pe.If(n > P + 32):
                        up(j, p, PASS)
                if ahead is not None:
                    turn_x(1 - j, p + 1, ahead)
                with pe.If(n < P + 1):
                    down(p, P)
                with pe.If(n > P):
                    down(p, PASS)

            pe.sem_inc(pe_done, 4)
            turn_x(0, 0, 0)
            with pe.Fori(0, E_N // 2 - 1) as h:
                for j in range(2):
                    pe_pass(j, h * 2 + j, h + j)
            pe_pass(0, E_N - 2, E_N // 2 - 1)
            pe_pass(1, E_N - 1, None)
            n = pe.value_load(over_row[0:1, 2:3], min_val=0, max_val=NOVER)
            with pe.Fori(0, NOVER) as q:
                with pe.If(q < n):
                    turn_x(0, q + E_N, q + E_N // 2)
                    up(0, q + E_N, PASS)
                    down(q + E_N, PASS)

        block = ctx.enter_context(nc.Block())

        @block.sync
        def _(sp):
            sp.dma_start(x_meta, meta_tokens).then_inc(x_landed[0], 16)
            for t in range(NTOK):
                sp.dma_start(x_in[t], x_rows[t * P:(t + 1) * P, :]).then_inc(x_landed[t + 1], 16)
            for n, src in enumerate(chunks):
                if n >= RING:
                    sp.wait_ge(*used_when(n - RING))
                for h, s in enumerate(src):
                    dst = std(n % RING) if len(src) == 1 else glu_view(n % RING)[:, h]
                    sp.dma_start(dst, s).then_inc(ring_landed[n % RING], 16)
            experts_sync(sp)

        @block.gpsimd
        def _(pool):
            cn = [0]

            def const(ins):
                ins.then_inc(consts_done, 1)
                cn[0] += 1

            def settle():
                pool.wait_ge(consts_done, cn[0])

            const(pool.memset(ident, 0.0))
            const(pool.memset(turn, 0.0))
            const(pool.memset(hide, 0.0))
            const(pool.memset(before, 1.0))
            const(pool.memset(ones, 1.0))
            const(pool.memset(sgn, 1.0))
            const(pool.memset(nsgn, 1.0))
            const(pool.memset(half_pi, math.pi / 2))
            const(pool.memset(zero1, 0.0))
            const(pool.memset(ss, 1.0))
            const(pool.iota(step_j, [[1, NCH]], 0, 0, allow_small_or_imprecise_dtypes=True))
            const(pool.iota(step_t[:, 0:STEP], [[-1, STEP]], STEP - 1, 0, allow_small_or_imprecise_dtypes=True))
            const(pool.iota(step_t[:, STEP:2 * STEP], [[1, STEP]], 1, 0, allow_small_or_imprecise_dtypes=True))
            settle()
            sel = pool.affine_select
            const(sel(out=ident, in_=ident, compare_op=ALU.not_equal, fill=1.0, base=0, pattern=[[-1, P]], channel_multiplier=1))
            const(sel(out=turn[:, 0:P], in_=turn[:, 0:P], compare_op=ALU.not_equal, fill=1.0, base=0, pattern=[[-1, P]], channel_multiplier=1))
            const(sel(out=turn[:, P:P + NS], in_=turn[:, P:P + NS], compare_op=ALU.not_equal, fill=1.0, base=-NS, pattern=[[-1, NS]], channel_multiplier=1))
            const(sel(out=turn[:, P + NS:2 * P], in_=turn[:, P + NS:2 * P], compare_op=ALU.not_equal, fill=-1.0, base=0, pattern=[[-1, NS]], channel_multiplier=1))
            const(sel(out=before, in_=before, compare_op=ALU.is_gt, fill=0.0, base=0, pattern=[[1, P]], channel_multiplier=-1))
            const(sel(out=hide[:, 0:P], in_=hide[:, 0:P], compare_op=ALU.is_gt, fill=HIDE, base=0, pattern=[[1, P]], channel_multiplier=-1))
            const(sel(out=hide[:, P:2 * P], in_=hide[:, P:2 * P], compare_op=ALU.is_ge, fill=HIDE, base=0, pattern=[[-1, P]], channel_multiplier=1))
            const(sel(out=sgn, in_=sgn, compare_op=ALU.is_ge, fill=-1.0, base=NS - 1, pattern=[[0, 1]], channel_multiplier=-1))
            const(sel(out=nsgn, in_=nsgn, compare_op=ALU.is_ge, fill=-1.0, base=-NS, pattern=[[0, 1]], channel_multiplier=1))
            const(pool.memset(v_rows[:, 0, :], 0.0))
            settle()
            for k in k_T:
                const(pool.memset(k[0:HD, META:META + P], 0.0))
                settle()
                const(pool.memset(k[HD:HD + 1, :], 0.0))
                settle()
            settle()
            for k in k_T:
                const(pool.memset(k[HD:HD + 1, META:META + P], HIDE))
            settle()

            def move_u(ft):
                r = NXT + len(PIECES) * (ft + 1) - 1
                pool.wait_ge(pre_drained[r % 4], r // 4 + 1)
                pool.dma_start(u_dram[ft], u_T[ft % 2]).then_inc(u_out[ft], 16)
                pool.wait_ge(u_out[ft], 16)
                for s in range(STEP):
                    pool.dma_start(U[s * GC:(s + 1) * GC, 8 * ft:8 * ft + 8, :],
                                   u_dram[ft, :, s, :].rearrange("(g c) j -> c g j", c=GC)).then_inc(u_moved[ft], 16)

            for ft in range(4):
                move_u(ft)

            step = pool_step
            pool.wait_ge(par_done, 1)
            for i in range(NB):
                gs = slice(i * BG, (i + 1) * BG)
                if i >= 1:
                    pool.wait_ge(cs_done, 2 * i)
                jj = bc(step_j, 1, BG)
                step.mark(pool.tensor_tensor(Pa, jj, bc(hi8[:, gs], 2, NCH), ALU.mult))
                pool.wait_ge(step.sem, step.now())
                step.mark(pool.tensor_scalar(Pk, Pa, 1 / (2 * math.pi), MAGIC, ALU.mult, ALU.add))
                step.mark(pool.tensor_tensor(Pr, jj, bc(lo8[:, gs], 2, NCH), ALU.mult))
                pool.wait_ge(step.sem, step.now())
                step.mark(pool.tensor_scalar(Pk, Pk, MAGIC, -TWO_PI_HI, ALU.subtract, ALU.mult))
                pool.wait_ge(step.sem, step.now())
                step.mark(pool.tensor_tensor(Pa, Pa, Pk, ALU.add))
                pool.wait_ge(step.sem, step.now())
                step.mark(pool.tensor_tensor(Pa, Pa, Pr, ALU.add))
                step.mark(pool.tensor_scalar(Pk, Pk, TWO_PI_LO / TWO_PI_HI, None, ALU.mult))
                pool.wait_ge(step.sem, step.now())
                step.mark(pool.tensor_tensor(Pa, Pa, Pk, ALU.add))
                pool.wait_ge(step.sem, step.now())
                pool.tensor_scalar(Pr, Pa, 3.1415925, -3.1415925, ALU.min, ALU.max).then_inc(ang_ready, 1)
                if i >= 1:
                    pool.wait_ge(y_ready, i)
                pr, pi = (bc(t[:, gs, STEP:2 * STEP], 3, GC) for t in (ab_re, ab_im))
                k1, k2 = (bc(t[:, gs, :], 2, STEP) for t in (K1, K2))
                step.mark(pool.tensor_tensor(G1, pr, k1, ALU.mult))
                step.mark(pool.tensor_tensor(Gtmp, pi, k2, ALU.mult))
                pool.wait_ge(step.sem, step.now())
                step.mark(pool.tensor_tensor(G1, G1, Gtmp, ALU.add))
                step.mark(pool.tensor_tensor(G2, pr, k2, ALU.mult))
                pool.wait_ge(step.sem, step.now())
                step.mark(pool.tensor_tensor(Gtmp, pi, k1, ALU.mult))
                pool.wait_ge(step.sem, step.now())
                pool.tensor_tensor(G2, G2, Gtmp, ALU.subtract).then_inc(g_done, 1)

            pool.wait_ge(gelu_done, 4)
            for q in q_blk:
                step.mark(pool.memset(q[HD:HD + 1], 1.0))
            pool.wait_ge(step.sem, step.now())
            r = NKV + 15
            pool.wait_ge(pre_drained[r % 4], r // 4 + 1)
            pool.sem_inc(q_staged, 1)
            with pool.Fori(0, NTOK // 2) as it:
                for half in range(2):
                    pool.wait_ge(s_ready, it * 32 + HEADS * (half + 1))
                    cs = bass.ds((it * 2 + half) * P, P)
                    for odd in range(2):
                        pool.wait_ge(q_staged, it * 4 + 2 * half + odd + 1)
                        pool.tensor_copy(q_blk[half][0:HD, odd:HEADS:2, :], q_T[odd * HD:(odd + 1) * HD, :, cs]).then_inc(q_staged, 1)
            experts_pool(pool)

        @block.scalar
        def _(act):
            sq = lambda a: a.rearrange("l a b -> (l a) b")
            par = []
            for h in range(2):
                par.append((raw_ar[:, h * NS:(h + 1) * NS], sq(ssm_a_re)))
                par.append((raw_ai[:, h * NS:(h + 1) * NS], sq(ssm_a_im)))
            par.append((raw_dt, ssm_log_dt.partition_broadcast(P).rearrange("p l g -> p (l g)")))
            for n, s in enumerate((ssm_b_re, ssm_b_im)):
                s = s.rearrange("l g p c -> p (l g) c")
                par.append((raw_b1[n * NS:(n + 1) * NS], s))
                par.append((raw_b2[(1 - n) * NS:(2 - n) * NS], s))
            for n, s in enumerate((ssm_c_re, ssm_c_im)):
                s = s.rearrange("l (a g) c p -> (g c) (l a) p", a=4)
                par.append((raw_c1[:, :, n * NS:(n + 1) * NS], s))
                par.append((raw_c2[:, :, (1 - n) * NS:(2 - n) * NS], s))
            for s in range(STEP):
                par.append((raw_d[:, s, :], ssm_d.rearrange("l (g c) -> (l g) c", c=GC)))
            for dst, src in par:
                act.dma_start(dst, src).then_inc(par_landed, 16)
            act.dma_start(mix_g, mix_norm_g.rearrange("l (k p) -> p (l k)", p=P), allow_slow_non_contiguous=True).then_inc(g_landed, 16)
            act.dma_start(sinks, attn_sinks.partition_broadcast(P).rearrange("p l h -> p (l h)")).then_inc(g_landed, 16)
            act.wait_ge(consts_done, 10)
            act.wait_ge(par_landed, 16 * len(par))
            act.activation(dt_, raw_dt, ACT.Exp).then_inc(dt_done, 1)
            act.wait_ge(pow_ready, 1)
            act.activation(ph[0], ph[0], ACT.Exp).then_inc(pow_done, 1)
            act.activation(ph[1], ph[1], ACT.Sin).then_inc(pow_done, 1)
            act.activation(ph[2], ph[2], ACT.Sin, bias=half_pi, scale=-1.0).then_inc(pow_done, 1)

            for t in range(NTOK + 1):
                n = META if t == 0 else P
                act.wait_ge(x_landed[t], 16)
                if t >= 1:
                    act.wait_ge(squares_done, t)
                act.activation(junk[0:n], x_meta if t == 0 else x_in[t - 1], ACT.Square,
                               accum_out=ss[0:n, t:t + 1]).then_inc(squares_done, 1)
            act.wait_ge(var_done, 1)
            act.activation(rstd, nw1, ACT.Sqrt).then_inc(root_done, 1)
            r = NXT
            for ft in range(4):
                if ft >= 2:
                    act.wait_ge(u_out[ft - 2], 16)
                for c0, n in PIECES:
                    act.wait_ge(pre_ready, r + 1)
                    act.activation(u_T[ft % 2][:, :, c0 // STEP:(c0 + n) // STEP],
                                   pre_bank(r)[:, 0:n].rearrange("p (j s) -> p s j", s=STEP), ACT.Copy)\
                       .then_inc(pre_drained[r % 4], 1)
                    r += 1
            for c0, n, d0 in ((0, META, 0), (0, 512, META + P), (512, 512, META + P + 512)):
                act.wait_ge(pre_ready, r + 1)
                for h in range(2):
                    ins = act.activation(k_T[h][0:HD, d0:d0 + n], pre_bank(r)[h * HD:(h + 1) * HD, 0:n], ACT.Copy)
                ins.then_inc(pre_drained[r % 4], 1)
                r += 1
            act.wait_ge(pre_ready, r + 1)
            act.activation(v_meta[0:META], pre_bank(r)[0:META, 0:P], ACT.Copy).then_inc(pre_drained[r % 4], 1)
            r += 1
            for h in range(2):
                act.wait_ge(pre_ready, r + 1)
                act.activation(v_rows[:, 1 + 4 * h:5 + 4 * h, :].rearrange("p a b -> p (a b)"), pre_bank(r)[:, :], ACT.Copy)\
                   .then_inc(pre_drained[r % 4], 1)
                r += 1

            def queries(n, r):
                act.wait_ge(pre_ready, r + 1)
                act.activation(q_T[:, n // 2, (n % 2) * 512:(n % 2 + 1) * 512], pre_bank(r)[:, :], ACT.Copy,
                               scale=-1.0 / 8).then_inc(pre_drained[r % 4], 1)

            def fetch_y(ft):
                act.dma_start(y_T[:, ft], y_dram[ft]).then_inc(y_moved[ft], 16)

            def outputs(i):
                act.wait_ge(y_ready, i + 1)
                if i >= 2 and i % 2 == 0:
                    act.wait_ge(y_out[i // 2 - 1], 16 * STEP)
                    fetch_y(i // 2 - 1)
                act.activation(Ysb[:, (i % 2) * BG:(i % 2 + 1) * BG, :].rearrange("p a b -> p (a b)"), bank[0][:, :], ACT.Copy)\
                   .then_inc(y_drained, 1)
                if i % 2:
                    ft = i // 2
                    act.wait_ge(y_drained, i + 1)
                    if i == 1:
                        for f in (2, 3):
                            act.wait_ge(u_out[f], 16)
                    for s in range(STEP):
                        act.dma_start(y_dram[ft, :, s, :].rearrange("(g c) j -> c g j", c=GC),
                                      Ysb[s * GC:(s + 1) * GC, :, :]).then_inc(y_out[ft], 16)

            for i in range(NB):
                queries(2 * i, r + 2 * i)
                act.wait_ge(ang_ready, i + 1)
                if i >= 1:
                    act.wait_ge(pq_done, i)
                act.activation(Pk, Pr, ACT.Abs).then_inc(abs_done, 1)
                act.activation(Sj, Pr, ACT.Sin).then_inc(cs_done, 1)
                act.wait_ge(abs_done, i + 1)
                act.activation(Cj, Pk, ACT.Sin, bias=half_pi, scale=-1.0).then_inc(cs_done, 1)
                if i >= 1:
                    outputs(i - 1)
                queries(2 * i + 1, r + 2 * i + 1)
            outputs(NB - 1)
            act.wait_ge(y_out[3], 16 * STEP)
            fetch_y(3)
            for ft in range(4):
                act.wait_ge(y_moved[ft], 16)
            for ft in range(4):
                act.activation(gy_T[:, ft, :].rearrange("p (j s) -> p s j", s=STEP), y_T[:, ft],
                               ACT.Gelu_apprx_tanh).then_inc(gelu_done, 1)
            act_attention(act)
            act_merge(act)
            experts_act(act)

        @block.vector
        def _(dve):
            step = dve_step

            def link(ins):
                step.mark(ins)
                dve.wait_ge(step.sem, step.now())

            dve.wait_ge(consts_done, 22)
            dve.wait_ge(par_turned, 3)
            link(dve.tensor_copy(a_re, bank[0][:, 0:G]))
            link(dve.tensor_copy(a_im, bank[0][:, G:2 * G]))
            link(dve.tensor_copy(skip_d, bank[0][:, 2 * G:3 * G]))
            k1f, k2f = (t.rearrange("p a b -> p (a b)") for t in (K1, K2))
            link(dve.tensor_scalar(k1f, bank[1][:, :], sgn, None, ALU.mult))
            link(dve.tensor_scalar(k2f, bank[2][:, :], -1.0, None, ALU.mult))
            link(dve.tensor_scalar(raw_b2, raw_b2, nsgn, None, ALU.mult))
            dve.wait_ge(dt_done, 1)
            link(dve.tensor_tensor(zz, a_re, dt_, ALU.mult))
            link(dve.tensor_tensor(c1, a_im, dt_, ALU.mult))

            def less_turns(r, ang, k):
                link(dve.tensor_scalar(k, ang, 1 / (2 * math.pi), MAGIC, ALU.mult, ALU.add))
                link(dve.tensor_scalar(k, k, MAGIC, None, ALU.subtract))
                link(dve.scalar_tensor_tensor(r, k, -TWO_PI_HI, ang, ALU.mult, ALU.add))
                link(dve.scalar_tensor_tensor(r, k, -TWO_PI_LO, r, ALU.mult, ALU.add))

            def split(hi, lo, r):
                link(dve.tensor_scalar(hi, r, SPLIT, None, ALU.add))
                link(dve.tensor_scalar(hi, hi, SPLIT, None, ALU.subtract))
                link(dve.tensor_tensor(lo, r, hi, ALU.subtract))

            less_turns(thr, c1, c2)
            split(hi1, lo1, thr)
            tt = bc(step_t, 1, G)
            link(dve.tensor_tensor(ph[0], tt, bc(zz, 2, 2 * STEP), ALU.mult))
            link(dve.tensor_tensor(ph[1], tt, bc(hi1, 2, 2 * STEP), ALU.mult))
            link(dve.tensor_tensor(ph[2], tt, bc(lo1, 2, 2 * STEP), ALU.mult))
            link(dve.tensor_scalar(ph[3], ph[1], 1 / (2 * math.pi), MAGIC, ALU.mult, ALU.add))
            link(dve.tensor_scalar(ph[3], ph[3], MAGIC, None, ALU.subtract))
            link(dve.scalar_tensor_tensor(ph[1], ph[3], -TWO_PI_HI, ph[1], ALU.mult, ALU.add))
            link(dve.tensor_tensor(ph[1], ph[1], ph[2], ALU.add))
            link(dve.scalar_tensor_tensor(ph[1], ph[3], -TWO_PI_LO, ph[1], ALU.mult, ALU.add))
            link(dve.tensor_copy(c1, ph[1][:, :, 2 * STEP - 1]))
            link(dve.tensor_scalar(ph[2], ph[1], -1.0, None, ALU.mult))
            link(dve.tensor_tensor(ph[2], ph[2], ph[1], ALU.max))
            dve.tensor_scalar(ph[1], ph[1], 3.1415925, -3.1415925, ALU.min, ALU.max).then_inc(pow_ready, 1)
            split(hi8, lo8, c1)
            dve.wait_ge(pow_done, 3)
            link(dve.tensor_tensor(ab_re, ph[0], ph[2], ALU.mult))
            link(dve.tensor_tensor(ab_im, ph[0], ph[1], ALU.mult))
            link(dve.tensor_tensor(c1, a_re, a_re, ALU.mult))
            link(dve.tensor_tensor(c2, a_im, a_im, ALU.mult))
            link(dve.tensor_scalar(c3, ab_re[:, :, STEP], 1.0, None, ALU.subtract))
            link(dve.tensor_tensor(c1, c1, c2, ALU.add))
            link(dve.reciprocal(thr, c1))
            link(dve.tensor_tensor(c1, c3, a_re, ALU.mult))
            link(dve.tensor_tensor(c2, ab_im[:, :, STEP], a_im, ALU.mult))
            link(dve.tensor_tensor(c1, c1, c2, ALU.add))
            link(dve.tensor_tensor(c1, c1, thr, ALU.mult))
            link(dve.tensor_tensor(c2, ab_im[:, :, STEP], a_re, ALU.mult))
            link(dve.tensor_tensor(c4, c3, a_im, ALU.mult))
            link(dve.tensor_tensor(c2, c2, c4, ALU.subtract))
            link(dve.tensor_tensor(c2, c2, thr, ALU.mult))
            cre, cim = bc(c1, 2, GC), bc(c2, 2, GC)
            p3, p4 = ph[3], ph[4]
            link(dve.tensor_tensor(B1, cre, raw_b1, ALU.mult))
            link(dve.tensor_tensor(p3, cim, raw_b2, ALU.mult))
            link(dve.tensor_tensor(B2, cre, raw_b2, ALU.mult))
            link(dve.tensor_tensor(p4, cim, raw_b1, ALU.mult))
            link(dve.tensor_tensor(B1, B1, p3, ALU.add))
            link(dve.tensor_tensor(B2, B2, p4, ALU.subtract))
            dve.wait_ge(g_landed, 32)
            link(dve.tensor_scalar(nsinks, sinks, -1.0, None, ALU.mult))
            link(dve.memset(Wrev[:, :, STEP:, :], 0.0))
            dve.tensor_copy(c3, ph[0][:, :, 2 * STEP - 1]).then_inc(par_done, 1)

            dve.wait_ge(squares_done, NTOK + 1)
            link(dve.tensor_scalar(nw1, ss, 1.0 / D, EPS, ALU.mult, ALU.add))
            dve.memset(nw2, 0.0).then_inc(var_done, 1)
            dve.wait_ge(root_done, 1)
            link(dve.reciprocal(rstd, rstd))
            newton(dve, link, rstd, nw1, nw2)
            for t in range(NTOK + 1):
                v, n = (x_meta, META) if t == 0 else (x_in[t - 1], P)
                dve.tensor_scalar(v, v, rstd[0:n, t:t + 1], None, ALU.mult).then_inc(hn_rows_done, 1)
            for r in range(NXT):
                dve.wait_ge(pre_ready, r + 1)
                if r == 0:
                    dst, src, g = hn_T[:, :, 0:META], pre_bank(r)[:, 0:KT * META].rearrange("p (k n) -> p k n", n=META), bc(mix_g, 2, META)
                else:
                    t, c = divmod(r - 1, 2)
                    dst = hn_T[:, 4 * c:4 * c + 4, META + t * P:META + (t + 1) * P]
                    src, g = pre_bank(r)[:, :].rearrange("p (k n) -> p k n", n=P), bc(mix_g[:, 4 * c:4 * c + 4], 2, P)
                dve.tensor_tensor(dst, src, g, ALU.mult).then_inc(pre_drained[r % 4], 1)

            def matrices(i):
                gs = slice(i * BG, (i + 1) * BG)
                if i >= 1:
                    dve.wait_ge(et_ready, BG * i)
                step.mark(dve.tensor_tensor(Wrev[:, :, 0:STEP, :], bc(ab_re[:, gs, 0:STEP], 3, GC), bc(B1[:, gs, :], 2, STEP), ALU.mult))
                link(dve.tensor_tensor(Wtmp, bc(ab_im[:, gs, 0:STEP], 3, GC), bc(B2[:, gs, :], 2, STEP), ALU.mult))
                dve.tensor_tensor(Wrev[:, :, 0:STEP, :], Wrev[:, :, 0:STEP, :], Wtmp, ALU.add).then_inc(w_done, 1)

            dve.wait_ge(par_done, 1)
            matrices(0)
            for i in range(NB):
                for g in range(BG):
                    n = i * BG + g
                    dve.wait_ge(et_ready, n + 1)
                    if i >= 1 and g == 0:
                        dve.wait_ge(y_ready, i)
                    b = bank[g % 2]
                    step.mark(dve.tensor_copy(ET[:, g, 0:2 * P], b[:, 0:2 * P]))
                    dve.scalar_tensor_tensor(ET[:, g, 2 * P:3 * P], ident, skip_d[:, n:n + 1], b[:, 2 * P:3 * P],
                                             ALU.mult, ALU.add).then_inc(et_drained, 1)
                step.mark(dve.tensor_copy(decay, bc(c3[:, i * BG:(i + 1) * BG], 2, NCH)))
                dve.wait_ge(step.sem, step.now())
                step.mark(dve.memset(decay[:, :, 0:1], 0.0))
                if i + 1 < NB:
                    matrices(i + 1)
                dve.wait_ge(cs_done, 2 * i + 2)
                for pr in range(2):
                    dve.wait_ge(xs_ready, 2 * i + pr + 1)
                    gg = slice(2 * pr, 2 * pr + 2)
                    xr, xi = (bank[2 + q][:, 0:2 * NCH].rearrange("p (a b) -> p a b", b=NCH) for q in range(2))
                    step.mark(dve.tensor_tensor(Wj[:, gg, :], Cj[:, gg, :], xr, ALU.mult))
                    link(dve.tensor_tensor(Vj[:, gg, :], Sj[:, gg, :], xi, ALU.mult))
                    dve.tensor_tensor(Wj[:, gg, :], Wj[:, gg, :], Vj[:, gg, :], ALU.add).then_inc(xs_drained, 1)
                dve.wait_ge(xs_drained, 2 * i + 2)
                flat = lambda t: t.rearrange("p a b -> p (a b)")
                link(dve.tensor_tensor_scan(flat(Vj), flat(decay), flat(Wj), 0.0, ALU.mult, ALU.add))
                if i >= 1:
                    dve.wait_ge(y_ready, i)
                js = slice(MCH - 1, NCH - 1)
                step.mark(dve.tensor_tensor(Pj, Cj[:, :, js], Vj[:, :, js], ALU.mult))
                dve.tensor_tensor(Qj, Sj[:, :, js], Vj[:, :, js], ALU.mult).then_inc(pq_done, 1)
            dve_attention(dve, step, link)
            dve_merge(dve, step)
            experts_dve(dve)

        @block.tensor
        def _(pe):
            def take(name):
                n = chunk_of[name]
                pe.wait_ge(ring_landed[n % RING], 16 * len(chunks_of_slot(n)))

            pe.wait_ge(consts_done, 22)
            pe.wait_ge(par_landed, 16 * 21)
            pe.transpose(bank[0][:, 0:G], raw_ar, ident[0:G, 0:G])
            pe.transpose(bank[0][:, G:2 * G], raw_ai, ident[0:G, 0:G])
            pe.transpose(bank[0][:, 2 * G:3 * G], raw_d.rearrange("p a b -> p (a b)"), ident[0:G, 0:G]).then_inc(par_turned, 1)
            for n, raw in ((1, raw_c1), (2, raw_c2)):
                for a in range(4):
                    ins = pe.transpose(bank[n][:, a * P:(a + 1) * P], raw[:, a, :], ident)
                ins.then_inc(par_turned, 1)

            def group(r):
                if r >= 4:
                    pe.wait_ge(pre_drained[r % 4], r // 4)
                return pre_bank(r)

            for r in range(NXT):
                t, c = (0, 0) if r == 0 else (1 + (r - 1) // 2, (r - 1) % 2)
                pe.wait_ge(hn_rows_done, t + 1)
                b = group(r)
                for k in range(KT if r == 0 else 4):
                    if r == 0:
                        ins = pe.transpose(b[:, k * META:(k + 1) * META], x_meta[:, k * P:(k + 1) * P], ident[0:META, 0:META])
                    else:
                        kk = 4 * c + k
                        ins = pe.transpose(b[:, k * P:(k + 1) * P], x_in[t - 1][:, kk * P:(kk + 1) * P], ident)
                ins.then_inc(pre_ready, 1)
            pe.wait_ge(pre_drained[(NXT - 1) % 4], (NXT - 1) // 4 + 1)

            def project(r, w, c0, n, rhs):
                b = group(r)
                for k in range(KT):
                    ins = pe.matmul(b[:, 0:n], w[:, k, :], rhs[:, k, c0:c0 + n], start=(k == 0), stop=(k == KT - 1))
                ins.then_inc(pre_ready, 1)
                return ins

            r = NXT
            for ft in range(4):
                take(("u", ft // 2))
                for c0, n in PIECES:
                    project(r, slot(("u", ft // 2))[:, :, (ft % 2) * P:(ft % 2 + 1) * P], c0, n, hn_T)
                    r += 1
            take("kv")
            w = slot("kv")
            for c0, n in ((0, META), (META, 512), (META + 512, 512)):
                project(r, w[:, :, 0:P], c0, n, hn_T)
                r += 1
            b = group(r)
            for k in range(KT):
                ins = pe.matmul(b[0:META, 0:P], hn_T[:, k, 0:META], w[:, k, P:2 * P], start=(k == 0), stop=(k == KT - 1))
            ins.then_inc(pre_ready, 1)
            r += 1
            for h in range(2):
                b = group(r)
                for t in range(4):
                    c0 = META + (4 * h + t) * P
                    for k in range(KT):
                        ins = pe.matmul(b[:, t * P:(t + 1) * P], hn_T[:, k, c0:c0 + P], w[:, k, P:2 * P], start=(k == 0), stop=(k == KT - 1))
                ins.then_inc(pre_ready, 1)
                r += 1

            def queries(n):
                ft, h = divmod(n, 2)
                take(("q", ft // 2))
                project(NKV + n, slot(("q", ft // 2))[:, :, (ft % 2) * P:(ft % 2 + 1) * P], META + h * 512, 512, hn_T)

            def matrices(i):
                pe.wait_ge(w_done, i + 1)
                for g in range(BG):
                    n = i * BG + g
                    b = bank[g % 2]
                    if n >= 2:
                        pe.wait_ge(et_drained, n - 1)
                    if i >= 1 and g == 0:
                        pe.wait_ge(y_drained, i)
                    wf = Wrev[:, g].rearrange("p m c -> p (m c)")
                    pe.matmul(b[:, 0:2 * P], wf[:, 0:P], turn, start=True, stop=True)
                    for t in range(STEP):
                        a = (STEP - 1 - t) * GC
                        ins = pe.matmul(b[:, 2 * P + t * GC:2 * P + (t + 1) * GC], wf[:, a:a + P], K1[:, n, :], start=True, stop=True)
                    ins.then_inc(et_ready, 1)

            def chunk_inputs(i):
                for pr in range(2):
                    pe.wait_ge(et_drained, i * BG + 2 * pr + 2)
                    if 2 * i + pr >= 1:
                        pe.wait_ge(xs_drained, 2 * i + pr)
                    if i % 2 == 0 and pr == 0:
                        pe.wait_ge(u_moved[i // 2], 16 * STEP)
                    for g in (2 * pr, 2 * pr + 1):
                        n = i * BG + g
                        for q in range(2):
                            ins = pe.matmul(bank[2 + q][:, (g % 2) * NCH:(g % 2 + 1) * NCH], ET[:, g, q * P:(q + 1) * P], U[:, n, :], start=True, stop=True)
                    ins.then_inc(xs_ready, 1)

            def outputs(i):
                pe.wait_ge(pq_done, i + 1)
                pe.wait_ge(g_done, i + 1)
                pe.wait_ge(et_drained, (i + 1) * BG)
                for g in range(BG):
                    n = i * BG + g
                    o = bank[0][:, g * P:(g + 1) * P]
                    pe.matmul(o, ET[:, g, 2 * P:3 * P], U[:, n, MCH:NCH], start=True, stop=False)
                    pe.matmul(o, G1[:, g].rearrange("p t c -> p (t c)"), Pj[:, g, :], start=False, stop=False)
                    ins = pe.matmul(o, G2[:, g].rearrange("p t c -> p (t c)"), Qj[:, g, :], start=False, stop=True)
                ins.then_inc(y_ready, 1)

            for i in range(NB):
                queries(2 * i)
                if i >= 1:
                    outputs(i - 1)
                matrices(i)
                queries(2 * i + 1)
                chunk_inputs(i)
            outputs(NB - 1)

            pe.sem_inc(s_ready, 32)
            pe.sem_inc(pt_turned, 2)
            pe.sem_inc(pt_used, 2)
            pe.sem_inc(at_ready, 4)
            for r in range(NKV + 12, NKV + 16):
                pe.wait_ge(pre_drained[r % 4], r // 4 + 1)
            pe.wait_ge(consts_done, 29)
            pe.wait_ge(y_drained, NB)
            with pe.Fori(0, NTOK // 2) as it:
                def turn_back(half):
                    pe.wait_ge(o_rows, it * 4 + 2 * half + 2 + 2)
                    for c in range(2):
                        pe.wait_ge(at_free, it * 4 + 2 * half + c + 1)
                        for a in range(4):
                            f = o_sb[half].rearrange("p h d -> p (h d)")[:, (4 * c + a) * P:(4 * c + a + 1) * P]
                            ins = pe.transpose(bank[6 + c][:, a * P:(a + 1) * P], f, ident)
                        ins.then_inc(at_ready, 1)

                for i in range(32 + 3):
                    if i < 32:
                        half, h = divmod(i, HEADS)
                        if h == 0:
                            pe.wait_ge(q_staged, it * 4 + 2 * half + 2 + 1)
                        k = k_T[h // REP]
                        q = q_blk[half][0:HD + 1, h, :]
                        pe.wait_ge(s_done, it * 32 + i + 1)
                        pe.matmul(bank[i % 2][:, 0:2 * P], q, k[0:HD + 1, bass.ds((it * 2 + half) * P + META, 2 * P)], start=True, stop=True)
                        pe.matmul(bank[i % 2][:, 2 * P:2 * P + META], q, k[0:HD + 1, 0:META], start=True, stop=True).then_inc(s_ready, 1)
                    if 2 <= i < 34:
                        j = i - 2
                        pe.wait_ge(p_done, it * 32 + j + 1 + 2)
                        pe.wait_ge(pt_a, it * 32 + j + 1)
                        pe.wait_ge(pt_b, it * 32 + j + 1)
                        for a in range(2):
                            pe.transpose(bank[2 + j % 2][:, a * P:(a + 1) * P], p_sb[j % 2][:, a * P:(a + 1) * P], ident)
                        pe.transpose(bank[2 + j % 2][0:META, 2 * P:3 * P], p_sb[j % 2][:, 2 * P:2 * P + META], ident).then_inc(pt_turned, 1)
                    if i >= 3:
                        j = i - 3
                        half, h = divmod(j, HEADS)
                        g = h // REP
                        pe.wait_ge(pt_a, it * 32 + j + 1 + 2)
                        pe.wait_ge(pt_b, it * 32 + j + 1 + 2)
                        if h % REP == 0:
                            pe.wait_ge(o_rows, it * 4 + j // REP + 1)
                        o = bank[4 + g % 2][:, (h % REP) * HD:(h % REP + 1) * HD]
                        for a in range(2):
                            pe.matmul(o, pt_sb[j % 2][:, a * P:(a + 1) * P],
                                      v_rows[:, bass.ds(it * 2 + half + a, 1), g * HD:(g + 1) * HD].rearrange("p a d -> p (a d)"), start=(a == 0), stop=False)
                        ins = pe.matmul(o, pt_sb[j % 2][0:META, 2 * P:3 * P], v_meta[0:META, g * HD:(g + 1) * HD], start=False, stop=True)
                        ins.then_inc(pt_used, 1)
                    if i == 24:
                        turn_back(0)
                turn_back(1)

            pe.wait_ge(gelu_done, 4)
            pe.wait_ge(at_free, 2 * NTOK + 2)
            for c in range(4):
                for kind, (name, rhs, c0) in enumerate(((("gs", c), hn_T, META), (("glu", c), gy_T, 0), (("glu", c), gy_T, 0),
                                                        (("ga", c), hn_T, META), (("ao", c), q_T, 0))):
                    take(name)
                    s = chunk_of[name] % RING
                    for g in range(4):
                        u = c * 20 + kind * 4 + g
                        if u >= 8:
                            pe.wait_ge(mix_drained[u % 8], u // 8)
                        w = glu_view(s)[:, 2 - kind] if name[0] == "glu" else std(s)
                        kt = w.shape[1]
                        f = (g // 2) * P
                        for k in range(kt):
                            ins = pe.matmul(bank[u % 8][:, :], w[:, k, f:f + P], rhs[:, k, c0 + (g % 2) * 512:c0 + (g % 2 + 1) * 512],
                                            start=(k == 0), stop=(k == kt - 1))
                        ins.then_inc(mix_ready, 1)
            experts_pe(pe)


_INS = ['x', 'meta_tokens', 'mix_norm_g', 'w_in', 'ssm_a_re', 'ssm_a_im', 'ssm_log_dt', 'ssm_b_re', 'ssm_b_im',
        'ssm_c_re', 'ssm_c_im', 'ssm_d', 'w_ssm_glu', 'attn_sinks', 'w_attn_o', 'w_out', 'ffn_norm_g',
        'router_w', 'router_b', 'w_up', 'b_up', 'w_down', 'b_down', 'final_norm_g']
_OUTS = [((1, 1024, 1024), 'float32')]


def kernel(**inputs):
    import numpy as _np
    import concourse.bacc as _bacc
    from concourse import mybir as _mybir
    from concourse.bass_utils import run_bass_kernel_spmd as _run

    nc = _bacc.Bacc("TRN2", target_bir_lowering=False, num_devices=1)
    arrays, args = {}, []
    for name in _INS:
        a = _np.ascontiguousarray(inputs[name])
        arrays[f"in_{name}_dram"] = a
        args.append(nc.dram_tensor(f"in_{name}_dram", a.shape, _mybir.dt.from_np(a.dtype), kind="ExternalInput").ap())
    for i, (shape, dtype) in enumerate(_OUTS):
        dt = _mybir.dt.from_np(_np.dtype(dtype))
        args.append(nc.dram_tensor(f"out_{i}_dram", shape, dt, kind="ExternalOutput").ap())
    build_trunk(nc, *args)
    r = _run(nc, [arrays], core_ids=[0])
    return r.results[0]["out_0_dram"]
```

```python
import math
from contextlib import ExitStack

import concourse.bass as bass
from concourse import mybir

P = 128
F32 = mybir.dt.float32
F32R = mybir.dt.float32r
I32 = mybir.dt.int32
U32 = mybir.dt.uint32
ALU = mybir.AluOpType
ACT = mybir.ActivationFunctionType
AX_X = mybir.AxisListType.X

D = 1024
SEQ = 1024
META = 16
LEN = SEQ + META
KT = D // P
NTOK = SEQ // P
SSM_W = 512
G = 32
GC = 16
NS = 64
STEP = 8
NCH = LEN // STEP
MCH = META // STEP
OCH = NCH - MCH
HEADS = 16
HD = 64
REP = 8
E_N = 32
FF = 1024
EPS = 1e-5
LIMIT = 7.0
ALPHA = 1.702
HIDE = 1e30

CH = 256
RING = 4
CHW = KT * CH

PASS = 192
PB = PASS - P
REGION = PASS * (-(-SEQ // PASS))
NOVER = (4 * SEQ) // PASS + 1
OVER_PAIRS = (NOVER + 1) // 2
NI = REGION // PASS - 1
UP_CH = 8
DN_CH = 4

TWO_PI_HI = 6.28125
TWO_PI_LO = 2 * math.pi - 6.28125
MAGIC = 1.5 * 2.0 ** 23
SPLIT = 1.5 * 2.0 ** 13


class Tally:

    def __init__(self, sem):
        self.sem, self.n, self.trip, self.per = sem, 0, None, 0

    def mark(self, ins, by=1):
        ins.then_inc(self.sem, by)
        self.n += by

    def now(self):
        return self.n if self.trip is None else self.trip * self.per + self.n

    def enter(self, trip, per):
        self.trip, self.per, self.start = trip, per, self.n

    def leave(self, trips):
        assert self.n - self.start == self.per, (self.n - self.start, self.per)
        self.n = self.start + self.per * trips
        self.trip = None


class Words:

    def __init__(self, t, size):
        self.t, self.size, self.at = t, size, 0

    def take(self, *shape, at=None, parts=P):
        n = math.prod(shape)
        a = self.at if at is None else at
        if at is None:
            self.at += n
        assert a + n <= self.size, (a, n, self.size)
        v = self.t[0:parts, a:a + n]
        if len(shape) == 2:
            v = v.rearrange("p (a b) -> p a b", b=shape[1])
        elif len(shape) == 3:
            v = v.rearrange("p (a b c) -> p a b c", b=shape[1], c=shape[2])
        return v


def bc(ap, axis, n):
    v = ap.unsqueeze(axis)
    return v.broadcast_to(list(v.shape[:axis]) + [n] + list(v.shape[axis + 1:]))


def build_trunk(nc, x, meta_tokens, mix_norm_g, w_in, ssm_a_re, ssm_a_im, ssm_log_dt, ssm_b_re, ssm_b_im,
                ssm_c_re, ssm_c_im, ssm_d, w_ssm_glu, attn_sinks, w_attn_o, w_out, ffn_norm_g,
                router_w, router_b, w_up, b_up, w_down, b_down, final_norm_g, out):
    x_rows = x.rearrange("b s d -> (b s) d")
    out_rows = out.rearrange("b s d -> (b s) d")

    def cols(w, c, n=CH):
        return w.rearrange("l (k p) f -> p (l k) f", p=P)[:, :, c:c + n]

    U0, Q0, K0, GS0, GA0 = 0, SSM_W, SSM_W + D, SSM_W + D + 256, SSM_W + D + 256 + D

    def std(s):
        return ring[:, s * CHW:(s + 1) * CHW].rearrange("p (k f) -> p k f", f=CH)

    def glu_view(s):
        return ring[:, s * CHW:(s + 1) * CHW].rearrange("p (h k f) -> p h k f", h=2, f=CH)

    chunk_of = {}
    chunks = []
    slot_of = []

    def add_chunk(name, *src, slot=None):
        chunk_of[name] = len(chunks)
        chunks.append(src)
        if slot is None:
            slot = (slot_of[-1] + 1) % RING if slot_of else 0
        slot_of.append(slot)

    for c in range(2):
        add_chunk(("u", c), cols(w_in, U0 + c * CH))
    add_chunk("kv", cols(w_in, K0))
    for c in range(4):
        add_chunk(("q", c), cols(w_in, Q0 + c * CH))
    for c in range(4):
        add_chunk(("gs", c), cols(w_in, GS0 + c * CH), slot=RING - 1)
        if c == 0:
            add_chunk(("glu", 0), cols(w_ssm_glu, 0), cols(w_ssm_glu, D))
            add_chunk(("ga", 0), cols(w_in, GA0))
            add_chunk(("ao", 0), cols(w_attn_o, 0))
    for c in range(1, 4):
        add_chunk(("glu", c), cols(w_ssm_glu, c * CH), cols(w_ssm_glu, D + c * CH), slot=RING - 1 if c == 1 else None)
        add_chunk(("ga", c), cols(w_in, GA0 + c * CH))
        add_chunk(("ao", c), cols(w_attn_o, c * CH))
    for c in range(4):
        add_chunk(("out", c), cols(w_out, c * CH))
    NPRE = len(chunks)
    names = {n: name for name, n in chunk_of.items()}

    with ExitStack() as ctx:
        def sem(name):
            return ctx.enter_context(nc.semaphore(name))

        def sems(name, n):
            return [sem(f"{name}{i}") for i in range(n)]

        bank = [ctx.enter_context(nc.psum_tensor(f"bank{i}", [P, 512], F32)) for i in range(8)]
        ring = ctx.enter_context(nc.sbuf_tensor("ring", [P, RING * CHW], F32))
        ring = ring[:, :]

        NCONST = 1800
        const_t = ctx.enter_context(nc.sbuf_tensor("consts", [P, NCONST], F32))
        cw = Words(const_t, NCONST)
        ident = cw.take(P)
        turn = cw.take(2 * P)
        hide = cw.take(META + 2 * P)
        before = cw.take(P)
        ones = cw.take(P)
        step_j = cw.take(NCH)
        step_t = cw.take(2 * STEP)
        sgn = cw.take(1)
        nsgn = cw.take(1)
        half_pi = cw.take(1)
        spare = cw.take(2)
        mix_g = cw.take(KT)
        sinks = cw.take(HEADS)
        nsinks = cw.take(HEADS)
        ss = cw.take(NTOK + 1)
        rstd = cw.take(NTOK + 1)
        nw1 = cw.take(NTOK + 1)
        nw2 = cw.take(NTOK + 1)

        NARENA = 43200
        arena_ctx = ExitStack()
        arena_t = arena_ctx.enter_context(nc.sbuf_tensor("arena", [P, NARENA], F32))
        ar = Words(arena_t, NARENA)
        hn_T = ar.take(KT, LEN)
        b_at = ar.at
        q_T = ar.take(KT, SEQ)
        u_at = ar.at
        U = ar.take(G, NCH)
        k_T = [ar.take(META + P + SEQ) for _ in range(2)]
        v_rows = ar.take(NTOK + 1, P)
        v_meta = ar.take(P)
        free_at = ar.at
        u_T = [ar.take(STEP, NCH) for _ in range(2)]
        y_T = ar.take(4, STEP, OCH, at=free_at)[:, :, :, :]
        ar.at = free_at + max(2 * STEP * NCH, 4 * STEP * OCH)
        Ysb = ar.take(8, OCH)
        a_re, a_im, dt_, zz, thr, hi1, lo1, hi8, lo8, skip_d = (ar.take(G) for _ in range(10))
        c1, c2, c3, c4 = (ar.take(G) for _ in range(4))
        ab_re = ar.take(G, 2 * STEP)
        ab_im = ar.take(G, 2 * STEP)
        B1, B2 = ar.take(G, GC), ar.take(G, GC)
        K1, K2 = ar.take(G, GC), ar.take(G, GC)
        par_at = ar.at
        raw_b1, raw_b2 = ar.take(G, GC), ar.take(G, GC)
        raw_c1, raw_c2 = ar.take(4, P), ar.take(4, P)
        raw_ar, raw_ai = ar.take(P, parts=G), ar.take(P, parts=G)
        raw_d = ar.take(STEP, GC, parts=G)
        raw_dt = ar.take(G)
        ph = [ar.take(G, 2 * STEP) for _ in range(5)]
        BG = 4
        NB = G // BG
        ar.at = par_at
        Cj, Sj, Pa, Pk, Pr = (ar.take(BG, NCH) for _ in range(5))
        decay, Wj, Vj = (ar.take(BG, NCH) for _ in range(3))
        Pj, Qj = ar.take(BG, OCH), ar.take(BG, OCH)
        Wrev = ar.take(BG, 2 * STEP - 1, GC)
        Wtmp = ar.take(BG, STEP, GC)
        ET = ar.take(BG, 3 * P)
        G1, G2, Gtmp = (ar.take(BG, STEP, GC) for _ in range(3))
        x_in = [ar.take(D, at=b_at + t * D) for t in range(NTOK)]
        x_meta = ar.take(D, at=u_at, parts=META)
        junk = ar.take(D, at=u_at + D)
        gy_T = ar.take(4, SEQ, at=u_at)
        m_T = ar.take(KT, SEQ, at=free_at)
        ar.at = par_at
        q_blk = [ar.take(HEADS, P) for _ in range(2)]
        s_sb = [ar.take(META + 2 * P) for _ in range(2)]
        p_sb = [ar.take(META + 2 * P) for _ in range(2)]
        pt_sb = [ar.take(3 * P) for _ in range(2)]
        o_sb = [ar.take(HEADS, HD) for _ in range(2)]
        nmax = [ar.take(HEADS) for _ in range(2)]
        rsum = [ar.take(HEADS) for _ in range(2)]
        esink = [ar.take(HEADS) for _ in range(2)]
        rden = [ar.take(HEADS) for _ in range(2)]
        ar.at = free_at + KT * SEQ
        assert par_at >= ar.at
        sg_b, sg_a, m_tmp = (ar.take(4, 512) for _ in range(3))
        u_dram = nc.dram_tensor("u_dram", (4, P, STEP, NCH), F32).ap()
        y_dram = nc.dram_tensor("y_dram", (4, P, STEP, OCH), F32).ap()
        arena_ctx.close()
        ring_landed = sems("ring_landed", RING)
        par_landed = sem("par_landed")
        g_landed = sem("g_landed")
        x_landed = sems("x_landed", NTOK + 1)
        consts_done = sem("consts_done")
        pool_step = Tally(sem("pool_step"))
        dve_step = Tally(sem("dve_step"))
        squares_done = sem("squares_done")
        var_done = sem("var_done")
        root_done = sem("root_done")
        hn_rows_done = sem("hn_rows_done")
        pre_ready = sem("pre_ready")
        pre_drained = sems("pre_drained", 4)
        par_turned = sem("par_turned")
        dt_done = sem("dt_done")
        pow_ready = sem("pow_ready")
        pow_done = sem("pow_done")
        par_done = sem("par_done")
        ang_ready = sem("ang_ready")
        cs_done = sem("cs_done")
        abs_done = sem("abs_done")
        g_done = sem("g_done")
        w_done = sem("w_done")
        et_ready = sem("et_ready")
        et_drained = sem("et_drained")
        xs_ready = sem("xs_ready")
        xs_drained = sem("xs_drained")
        pq_done = sem("pq_done")
        y_ready = sem("y_ready")
        y_drained = sem("y_drained")
        u_out = sems("u_out", 4)
        u_moved = sems("u_moved", 4)
        y_out = sems("y_out", 4)
        y_moved = sems("y_moved", 4)
        gelu_done = sem("gelu_done")
        q_staged = sem("q_staged")
        s_ready = sem("s_ready")
        s_done = sem("s_done")
        p_done = sem("p_done")
        pt_turned = sem("pt_turned")
        pt_a = sem("pt_a")
        pt_b = sem("pt_b")
        pt_used = sem("pt_used")
        o_rows = sem("o_rows")
        sink_in = sem("sink_in")
        sink_out = sem("sink_out")
        at_ready = sem("at_ready")
        at_free = sem("at_free")
        mix_ready = sem("mix_ready")
        h_ready = sem("h_ready")
        mix_drained = sems("mix_drained", 8)
        gs_ready = sem("gs_ready")
        gs_done = sem("gs_done")
        gs_sig = sem("gs_sig")
        merged = sem("merged")

        def chunks_of_slot(n):
            return [s for m in range(n + 1) if slot_of[m] == slot_of[n] for s in chunks[m]]

        def used_when(n):
            name = names[n]
            if name == "kv":
                return pre_ready, NKV
            kind, c = name
            return {"u": (pre_ready, NXT + 6 * (c + 1)), "q": (pre_ready, NKV + 4 * (c + 1)),
                    "gs": (gs_ready, 4 * (c + 1)),
                    "glu": (mix_ready, 16 * c + 8), "ga": (mix_ready, 16 * c + 12), "ao": (mix_ready, 16 * c + 16),
                    "out": (h_ready, 2 * NTOK)}[kind]

        def slot(name):
            return std(slot_of[chunk_of[name]])

        def pre_bank(r):
            return bank[4 + r % 4]

        NXT = 2 * NTOK + 1
        PIECES = [(0, 352), (352, 344), (696, 344)]
        NU = NXT + 4 * len(PIECES)
        NKV = NU + 6

        GS_STEPS = {i: [] for i in range(HEADS * 2 + 3)}
        for n, steps in enumerate((list(range(3, 11)), list(range(11, 19)), [19, 19, 20, 20, 21, 21, 22, 23], [28, 28, 29, 29, 30, 30, 31, 32])):
            for k, i in enumerate(steps):
                GS_STEPS[i].append((n, k))
        GS_STORE = [11, 19, 24, 33]

        def act_attention(act):
            act.wait_ge(gelu_done, 4)
            act.sem_inc(p_done, 2)
            act.sem_inc(pt_b, 2)
            act.sem_inc(at_free, 2)
            with act.Fori(0, NTOK // 2) as it:
                for i in range(32 + 4):
                    if i < 32:
                        half, h = divmod(i, HEADS)
                        act.wait_ge(s_done, it * 32 + i + 1 + 2)
                        act.wait_ge(pt_turned, it * 32 + i + 1)
                        act.activation(p_sb[i % 2], s_sb[i % 2], ACT.Exp, bias=nmax[half][:, h:h + 1], scale=-1.0,
                                       accum_out=rsum[half][:, h:h + 1]).then_inc(p_done, 1)
                    if 2 <= i < 34:
                        j = i - 2
                        act.wait_ge(pt_a, it * 32 + j + 1 + 2)
                        act.wait_ge(pt_used, it * 32 + j + 1)
                        act.activation(pt_sb[j % 2][0:META, 2 * P:3 * P], bank[2 + j % 2][0:META, 2 * P:3 * P], ACT.Copy)\
                           .then_inc(pt_b, 1)
                    if i % 8 == 2 and i > 8:
                        q8 = i // 8 - 1
                        half, hs = q8 // 2, slice((q8 % 2) * 8, (q8 % 2) * 8 + 8)
                        act.wait_ge(sink_in, it * 4 + q8 + 1)
                        act.activation(esink[half][:, hs], esink[half][:, hs], ACT.Exp).then_inc(sink_out, 1)
                    if i in GS_STORE:
                        n = GS_STORE.index(i)
                        act.wait_ge(gs_ready, it * 4 + n + 1)
                        act.activation(m_T[:, bass.ds(it * 2 + n // 2, 1), (n % 2) * 512:(n % 2 + 1) * 512].rearrange("p a b -> p (a b)"),
                                       bank[6 + n % 2][:, :], ACT.Copy).then_inc(gs_done, 1)
                    if i == 26:
                        turned(act, it, 0)
                turned(act, it, 1)

        def turned(act, it, half):
            for c in range(2):
                act.wait_ge(at_ready, it * 4 + half * 2 + c + 1 + 4)
                act.activation(q_T[:, 4 * c:4 * c + 4, bass.ds((it * 2 + half) * P, P)],
                               bank[6 + c][:, :].rearrange("p (a b) -> p a b", b=P), ACT.Copy).then_inc(at_free, 1)

        def act_merge(act):
            act.wait_ge(gs_done, 16)
            for c in range(4):
                m = m_T[:, 2 * c:2 * c + 2, :]
                act.activation(m, m, ACT.Sigmoid).then_inc(gs_sig, 1)
                for kind, dst in ((0, sg_b), (2, sg_a)):
                    for g in range(4):
                        u = c * 16 + kind * 4 + g
                        act.wait_ge(mix_ready, u + 1)
                        if c >= 1 and kind == 0 and g == 0:
                            v = (c - 1) * 16 + 7
                            act.wait_ge(mix_drained[v % 8], v // 8 + 1)
                        if c >= 1 and kind == 2 and g == 0:
                            act.wait_ge(merged, 4 * c)
                        act.activation(dst[:, g, :], bank[u % 8][:, :], ACT.Sigmoid).then_inc(mix_drained[u % 8], 1)

        def newton(dve, link, r, v, tmp):
            link(dve.tensor_tensor(tmp, r, r, ALU.mult))
            link(dve.tensor_tensor(tmp, tmp, v, ALU.mult))
            link(dve.tensor_scalar(tmp, tmp, -0.5, 1.5, ALU.mult, ALU.add))
            link(dve.tensor_tensor(r, r, tmp, ALU.mult))

        def dve_attention(dve, step, link):
            dve.wait_ge(gelu_done, 4)
            dve.sem_inc(s_done, 2)
            dve.sem_inc(pt_a, 2)
            dve.sem_inc(o_rows, 2)
            with dve.Fori(0, NTOK // 2) as it:
                step.enter(it, 8)
                for i in range(32 + 5):
                    if i < 32:
                        half, h = divmod(i, HEADS)
                        dve.wait_ge(s_ready, it * 32 + i + 1 + 32)
                        dve.wait_ge(p_done, it * 32 + i + 1)
                    if i < 2:
                        dve.memset(spare[:, i:i + 1], 0.0)
                    if 2 <= i < 34:
                        j = i - 2
                        dve.wait_ge(pt_turned, it * 32 + j + 1 + 2)
                        dve.wait_ge(pt_used, it * 32 + j + 1)
                        dve.tensor_copy(pt_sb[j % 2][:, 0:2 * P], bank[2 + j % 2][:, 0:2 * P]).then_inc(pt_a, 1)
                    if i < 32:
                        dve.tensor_tensor_reduce(s_sb[i % 2], bank[i % 2][:, 0:2 * P + META], hide, 1.0,
                                                 nsinks[:, h:h + 1], ALU.add, ALU.min, nmax[half][:, h:h + 1]).then_inc(s_done, 1)
                    if i % 8 == 1 and i > 8:
                        q8 = i // 8 - 1
                        half, hs = q8 // 2, slice((q8 % 2) * 8, (q8 % 2) * 8 + 8)
                        dve.wait_ge(s_done, it * 32 + 8 * q8 + 8 + 2)
                        dve.tensor_tensor(esink[half][:, hs], nmax[half][:, hs], sinks[:, hs], ALU.add).then_inc(sink_in, 1)
                    if i % 8 == 4 and i > 8:
                        q8 = i // 8 - 1
                        half, hs = q8 // 2, slice((q8 % 2) * 8, (q8 % 2) * 8 + 8)
                        dve.wait_ge(sink_out, it * 4 + q8 + 1)
                        dve.wait_ge(pt_used, it * 32 + 8 * q8 + 8 + 2)
                        link(dve.tensor_tensor(rden[half][:, hs], esink[half][:, hs], rsum[half][:, hs], ALU.add))
                        link(dve.reciprocal(rden[half][:, hs], rden[half][:, hs]))
                        dve.wait_ge(at_ready, it * 4 + half * 2 + 2)
                        dve.tensor_tensor(o_sb[half][:, hs, :], bank[4 + q8 % 2][:, :].rearrange("p (h d) -> p h d", d=HD),
                                          bc(rden[half][:, hs], 2, HD), ALU.mult).then_inc(o_rows, 1)
                step.leave(NTOK // 2)

        def dve_merge(dve, step):
            def drained(u):
                dve.wait_ge(mix_drained[u % 8], u // 8 + 1)

            dve.wait_ge(at_free, 2 * NTOK + 2)
            for c in range(4):
                drained(c * 16 + 3)
                dve.wait_ge(gs_sig, c + 1)
                step.mark(dve.tensor_tensor(sg_b, sg_b, m_T[:, 2 * c:2 * c + 2, :].rearrange("p a (h b) -> p (a h) b", h=2), ALU.mult))
                dve.wait_ge(step.sem, step.now())
                for g in range(4):
                    u = c * 16 + 4 + g
                    dve.wait_ge(mix_ready, u + 1)
                    m = m_T[:, 2 * c + g // 2, (g % 2) * 512:(g % 2 + 1) * 512]
                    dve.tensor_tensor(m, bank[u % 8][:, :], sg_b[:, g, :], ALU.mult).then_inc(mix_drained[u % 8], 1)
                for g in range(4):
                    u = c * 16 + 12 + g
                    m = m_T[:, 2 * c + g // 2, (g % 2) * 512:(g % 2 + 1) * 512]
                    drained(c * 16 + 8 + g)
                    dve.wait_ge(mix_ready, u + 1)
                    dve.tensor_tensor(m_tmp[:, g, :], bank[u % 8][:, :], sg_a[:, g, :], ALU.mult).then_inc(mix_drained[u % 8], 1)
                    drained(u)
                    dve.tensor_tensor(m, m, m_tmp[:, g, :], ALU.add).then_inc(merged, 1)

        rw_ = Words(arena_t, NARENA)
        h_rows = rw_.take(NTOK, D)
        hf_rows = [rw_.take(D) for _ in range(2)]
        hf_T = [rw_.take(KT, P) for _ in range(2)]
        ffn_g = rw_.take(D)
        h_junk = rw_.take(D)
        bdown = rw_.take(D, parts=E_N)
        assert rw_.at <= free_at
        SMALL = free_at + KT * SEQ
        rs = Words(arena_t, NARENA)
        rs.at = SMALL
        rout_w = rs.take(KT, E_N)
        rout_b = rs.take(E_N)
        h_ss, h_r, h_v, h_t = (rs.take(NTOK) for _ in range(4))
        logit = rs.take(NTOK, E_N)
        top_v = rs.take(NTOK, 8)
        top_e = rs.take(NTOK, 4)
        top_i = rs.take(NTOK * 8).bitcast(U32).rearrange("p (t k) -> p t k", k=8)
        expo, esum = rs.take(NTOK, 4), rs.take(NTOK)
        ntop = rs.take(NTOK)
        gate = rs.take(NTOK, 4)
        pick = rs.take(2, 4, E_N)
        pick_g = rs.take(4, E_N)
        pick_s = rs.take(4, E_N)
        picked = rs.take(NTOK, E_N)
        running = rs.take(NTOK + 1, E_N)
        gmat = rs.take(NTOK, E_N)
        gmat_T = rs.take(2, P, parts=E_N)
        place = rs.take(NTOK, E_N)
        slot_f = rs.take(NTOK, 4)
        e_iota, e_region = rs.take(E_N), rs.take(E_N)
        entry = rs.take(NTOK * 16)
        slot_i = rs.take(NTOK * 4).bitcast(I32)
        FILL = 96
        empty = rs.take(4 * FILL).bitcast(I32).rearrange("p (r f) -> p r f", f=4)
        NF = E_N * NI
        flag, cum, sel_q, base_f, exp_f, ones_f = (rs.take(NF) for _ in range(6))
        over_q = rs.take(1)
        over_v = rs.take(4)
        over_vi = rs.take(4).bitcast(I32)
        count_b = rs.take(E_N)
        over_row = rs.take(4 * P, parts=1).bitcast(I32)
        raw_bias = rs.take(4, P)
        bias_T = rs.take(E_N * 16)
        bias_now = [rs.take(16) for _ in range(2)]
        final_g = rs.take(D)
        entry_i = entry.bitcast(I32).rearrange("p (t k f) -> p t k f", k=4, f=4)
        entry_f = entry.rearrange("p (t k f) -> p t k f", k=4, f=4)

        def sb(name, shape, dt=F32):
            return ctx.enter_context(nc.sbuf_tensor(name, shape, dt))[:]

        WB = DN_CH
        ROWS = 2 * P
        W_AT = SMALL - 2 * WB * CHW
        a_hi, a_lo = (sb(f"a_{part}", [P, KT, ROWS], F32R) for part in ("hi", "lo"))
        ew = Words(arena_t, NARENA)
        ew.at = 2 * KT * ROWS
        sb("between", [P, W_AT - ew.at])
        w_hi, w_lo = ([sb(f"w_{part}{b}", [P, KT, CH], F32R) for b in range(WB)] for part in ("hi", "lo"))
        x_T = [ew.take(KT, PASS) for _ in range(2)]
        gat = [[ew.take(D), ew.take(D, parts=PB)] for _ in range(2)]
        y_sb = [[ew.take(D), ew.take(D, parts=PB)] for _ in range(2)]
        assert ew.at <= W_AT and rw_.at <= W_AT
        glu_s = [rs.take(2, PASS) for _ in range(2)]
        lin_s = [rs.take(2, PASS) for _ in range(2)]
        sig_s = [rs.take(2, PASS) for _ in range(2)]
        idx = [[rs.take(4).bitcast(I32), rs.take(4, parts=PB).bitcast(I32)] for _ in range(2)]
        FB = 4
        fw = Words(arena_t, NARENA)
        fin = [fw.take(4, D) for _ in range(FB)]
        fin_h = [ring[:, t * D:(t + 1) * D] for t in range(NTOK)]
        assert NTOK * D <= RING * CHW
        fin_junk = fw.take(D)
        fin_ss, fin_r, fin_v, fin_t = (fw.take(NTOK) for _ in range(4))
        assert fw.at <= SMALL

        NPASS = E_N + NOVER
        NSLOT = E_N * REGION
        hf_dram = nc.dram_tensor("hf_dram", (SEQ, D), F32).ap()
        h_dram = nc.dram_tensor("h_dram", (SEQ, D), F32).ap()
        y_rows_dram = nc.dram_tensor("y_rows_dram", (4 * SEQ, D), F32).ap()
        table = nc.dram_tensor("table", (NSLOT, 4), I32).ap()
        over_dram = nc.dram_tensor("over_dram", (P, 4), I32).ap()

        r_loads = sem("r_loads")
        h_added = sem("h_added")
        sq_done = sem("sq_done")
        v_done = sem("v_done")
        rt_done = sem("rt_done")
        hf_done = sem("hf_done")
        hf_stored = sems("hf_stored", 2)
        hf_turned = sem("hf_turned")
        hf_T_done = sem("hf_T_done")
        logits_ready = sem("logits_ready")
        exp_in = sem("exp_in")
        exp_out = sem("exp_out")
        picked_done = sem("picked_done")
        pos_ready = sem("pos_ready")
        place_done = sem("place_done")
        slot_done = sem("slot_done")
        bias_ready = sem("bias_ready")
        h2_added = sem("h2_added")
        h2_stored = sem("h2_stored")
        rc_done = sem("rc_done")
        filled = sem("filled")
        entered = sem("entered")
        bup_turned = sem("bup_turned")
        bup_done = sem("bup_done")
        counts_ready = sem("counts_ready")
        over_done = sem("over_done")
        over_out = sem("over_out")
        over_in = sem("over_in")
        ids_landed = sem("ids_landed")
        pool_passed = sem("pool_passed")
        gathered = sems("gathered", 2)
        scattered = sem("scattered")
        x_turned = sem("x_turned")
        x_stored = sem("x_stored")
        up_drained = sem("up_drained")
        sigm_done = sem("sigm_done")
        a_done = sem("a_done")
        y_done = sem("y_done")
        given = sem("given")
        pe_done = sem("pe_done")
        lo_done = sem("lo_done")
        hi_done = sem("hi_done")
        ah_done = sem("ah_done")
        a_cleared = sem("a_cleared")
        prod_done = sem("prod_done")
        bias_sem = sem("bias_sem")
        fin_step = sem("fin_step")
        experts_done = sem("experts_done")
        fin_landed = sems("fin_landed", FB)
        fg_landed = sem("fg_landed")
        fin_sum = sem("fin_sum")
        fin_sq = sem("fin_sq")
        fin_var = sem("fin_var")
        fin_root = sem("fin_root")
        fin_done = sem("fin_done")
        stored = sem("stored")

        row1 = lambda a: a.partition_broadcast(P).rearrange("p l d -> p (l d)")
        w_up_v = w_up.rearrange("l e (k p) f -> p (l e) k f", p=P)
        w_dn_v = w_down.rearrange("l e (k p) f -> p (l e) k f", p=P)

        def chunk_src(e, c):
            v, f = (w_up_v, (c % 2) * FF + (c // 2) * CH) if c < UP_CH else (w_dn_v, (c - UP_CH) * CH)
            return v[:, bass.ds(e, 1), :, f:f + CH].rearrange("p e k f -> p (e k) f")

        def landed(engine, p, c):
            s = c % RING
            before_it = sum(len(chunks[m]) for m in range(NPRE) if slot_of[m] == s)
            engine.wait_ge(ring_landed[s], p * 48 + 16 * (before_it + c // RING + 1))

        def experts_sync(sp):
            sp.wait_ge(mix_ready, 64)
            for t in range(NTOK):
                sp.dma_start(h_rows[:, t, :], x_rows[t * P:(t + 1) * P, :]).then_inc(x_landed[t + 1], 16)
            sp.dma_start(ffn_g, row1(ffn_norm_g)).then_inc(r_loads, 16)
            sp.dma_start(bdown, b_down.rearrange("l e d -> (l e) d")).then_inc(r_loads, 16)
            sp.wait_ge(merged, 16)
            sp.dma_start(rout_w, router_w.rearrange("l (k p) e -> p (l k) e", p=P)).then_inc(r_loads, 16)
            sp.dma_start(rout_b, row1(router_b)).then_inc(r_loads, 16)
            sp.dma_start(raw_bias, b_up.rearrange("l (a e) (t p) -> (e t) (l a) p", a=4, p=P)).then_inc(r_loads, 16)
            sp.dma_start(final_g, final_norm_g.partition_broadcast(P)).then_inc(fg_landed, 16)

            def pass_weights(e, p):
                for c in range(UP_CH + DN_CH):
                    if c < RING:
                        sp.wait_ge(lo_done, p * 4 + c + 1)
                    else:
                        sp.wait_ge(pe_done, p * 12 + c - RING + 1 + 4)
                    s = c % RING
                    sp.dma_start(std(s), chunk_src(e, c)).then_inc(ring_landed[s], 16)

            sp.wait_ge(h_ready, 2 * NTOK)
            with sp.Fori(0, E_N) as p:
                pass_weights(p, p)
            sp.wait_ge(over_in, 16)
            n = sp.value_load(over_row[0:1, 2:3], min_val=0, max_val=NOVER)
            with sp.If(n > 0):
                with sp.Fori(0, NOVER) as q:
                    with sp.If(q < n):
                        e = sp.value_load(over_row[0:1, bass.ds(q * 4 + 1, 1)], min_val=0, max_val=E_N - 1)
                        pass_weights(e, q + E_N)
            sp.wait_ge(lo_done, n * 4 + 4 * E_N + 4)
            for t in range(NTOK):
                sp.dma_start(fin_h[t], h_dram[t * P:(t + 1) * P, :]).then_inc(x_landed[t + 1], 16)
            sp.wait_ge(experts_done, 1)
            for t in range(NTOK):
                if t >= FB:
                    sp.wait_ge(fin_sum, t - FB + 1)
                sp.dma_start(fin[t % FB], y_rows_dram.rearrange("(k r) d -> r k d", k=4)[t * P:(t + 1) * P]).then_inc(fin_landed[t % FB], 16)
            sp.wait_ge(stored, 16 * NTOK)

        def experts_pool(pool):
            cn = [0]

            def const(ins):
                ins.then_inc(rc_done, 1)
                cn[0] += 1
                pool.wait_ge(rc_done, cn[0])

            pool.wait_ge(merged, 16)
            const(pool.iota(e_iota, [[1, E_N]], 0, 0, allow_small_or_imprecise_dtypes=True))
            const(pool.iota(e_region, [[REGION, E_N]], 0, 0, allow_small_or_imprecise_dtypes=True))
            const(pool.memset(running[:, 0, :], 0.0))
            const(pool.memset(entry_i[:, :, :, 3], 0))
            const(pool.iota(entry_i[:, :, :, 0], [[P, NTOK], [0, 4]], 0, 1))
            const(pool.iota(entry_i[:, :, :, 1], [[P, NTOK], [SEQ, 4]], 0, 1))
            const(pool.memset(empty, 0))
            const(pool.memset(empty[:, :, 1], 1 << 20))
            const(pool.memset(ones_f, 1.0))
            const(pool.iota(over_q, [[0, 1]], 1, 1, allow_small_or_imprecise_dtypes=True))
            const(pool.iota(exp_f.rearrange("p (i e) -> p i e", e=E_N), [[0, NI], [1, E_N]], 0, 0, allow_small_or_imprecise_dtypes=True))
            const(pool.iota(base_f.rearrange("p (i e) -> p i e", e=E_N), [[PASS, NI], [REGION, E_N]], PASS, 0, allow_small_or_imprecise_dtypes=True))
            NFILL = NSLOT // (P * FILL)
            for a in range(NFILL):
                pool.dma_start(table[a * P * FILL:(a + 1) * P * FILL, :].rearrange("(p r) f -> p r f", p=P), empty).then_inc(filled, 16)
            for s in range(NTOK + 4):
                if s < NTOK:
                    pool.wait_ge(hf_done, s + 1)
                    pool.dma_start(hf_dram[s * P:(s + 1) * P, :], hf_rows[s % 2]).then_inc(hf_stored[s % 2], 16)
                if s == 3:
                    pool.wait_ge(filled, 16 * NFILL)
                if s >= 4:
                    t = s - 4
                    pool.wait_ge(h2_added, 2 * t + 2)
                    pool.dma_start(h_dram[t * P:(t + 1) * P, :], h_rows[:, t, :]).then_inc(h2_stored, 16)
                if 3 <= s < NTOK + 3:
                    t = s - 3
                    pool.wait_ge(slot_done, t + 1)
                    for k in range(4):
                        pool.indirect_dma_start(table, bass.IndirectOffsetOnAxis(ap=slot_i[:, 4 * t + k:4 * t + k + 1], axis=0),
                                                entry_i[:, t, k, :], None, bounds_check=NSLOT - 1).then_inc(entered, 16)
            for b in range(2):
                pool.wait_ge(hf_stored[b], 16 * NTOK // 2)
            pool.wait_ge(h2_stored, 16 * NTOK)
            pool.wait_ge(entered, 64 * NTOK)

            def fetch(j, base, p):
                for b, n in ((0, P), (1, PB)):
                    pool.dma_start(idx[j][b], table[bass.ds(base + b * P, n), :]).then_inc(ids_landed, 16)
                pool.wait_ge(ids_landed, p * 32 + 32)
                pool.sem_inc(pool_passed, 1)
                for b, n in ((0, P), (1, PB)):
                    pool.indirect_dma_start(gat[j][b], None, hf_dram, bass.IndirectOffsetOnAxis(ap=idx[j][b][:, 0:1], axis=0),
                                            bounds_check=SEQ - 1).then_inc(gathered[j], 16)

            def give(j, p):
                pool.wait_ge(y_done, p * 2 + 2 + 2)
                pool.sem_inc(pool_passed, 1)
                for b, n in ((0, P), (1, PB)):
                    pool.indirect_dma_start(y_rows_dram, bass.IndirectOffsetOnAxis(ap=idx[j][b][:, 1:2], axis=0),
                                            y_sb[j][b], None, bounds_check=4 * SEQ - 1, oob_is_err=False).then_inc(scattered, 16)

            def fetch_next(j, p):
                pool.wait_ge(scattered, p * 32 + 32)
                pool.wait_ge(x_turned, p * 4 + 4)
                pool.sem_inc(given, 1)
                fetch(j, (p + 2) * REGION, p + 2)

            pool.sem_inc(given, 2)
            fetch(0, 0, 0)
            fetch(1, REGION, 1)
            with pool.Fori(0, E_N // 2 - 1) as h:
                for j in range(2):
                    give(j, h * 2 + j)
                    fetch_next(j, h * 2 + j)
            for j in range(2):
                give(j, E_N - 2 + j)
            pool.wait_ge(over_in, 16)
            pool.wait_ge(scattered, 32 * E_N)
            pool.sem_inc(given, 2)
            n = pool.value_load(over_row[0:1, 2:3], min_val=0, max_val=NOVER)
            with pool.If(n > 0):
                with pool.Fori(0, NOVER) as q:
                    with pool.If(q < n):
                        base = pool.value_load(over_row[0:1, bass.ds(q * 4, 1)], min_val=0, max_val=NSLOT - PASS)
                        fetch(0, base, q + E_N)
                        give(0, q + E_N)
                        pool.wait_ge(scattered, (q + E_N) * 32 + 32)
                        pool.sem_inc(given, 1)
            pool.wait_ge(scattered, n * 32 + 32 * E_N)
            pool.sem_inc(experts_done, 1)

        def experts_act(act):
            for s in range(NTOK + 3):
                if s < NTOK:
                    t = s
                    act.wait_ge(h_added, 2 * t + 2)
                    if t >= 1:
                        act.wait_ge(sq_done, t)
                    act.activation(h_junk, h_rows[:, t, :], ACT.Square, accum_out=h_ss[:, t:t + 1]).then_inc(sq_done, 1)
                    act.wait_ge(v_done, t + 1)
                    act.activation(h_r[:, t:t + 1], h_v[:, t:t + 1], ACT.Sqrt).then_inc(rt_done, 1)
                if 1 <= s <= NTOK:
                    t = s - 1
                    if t >= 2:
                        act.wait_ge(logits_ready, t - 1)
                    for c in range(2):
                        act.wait_ge(hf_turned, 2 * t + c + 1)
                        act.activation(hf_T[t % 2][:, 4 * c:4 * c + 4, :].rearrange("p a b -> p (a b)"), bank[4 + c][:, :], ACT.Copy)\
                           .then_inc(hf_T_done, 1)
                if 2 <= s < NTOK + 2:
                    t = s - 2
                    act.wait_ge(exp_in, t + 1)
                    act.activation(expo[:, t, :], top_v[:, t, 0:4], ACT.Exp, bias=ntop[:, t:t + 1],
                                   accum_out=esum[:, t:t + 1]).then_inc(exp_out, 1)

            def hi(p, d):
                landed(act, p, UP_CH + d)
                act.wait_ge(pe_done, p * 12 + d + 1)
                act.activation(w_hi[d], std((UP_CH + d) % RING), ACT.Copy).then_inc(hi_done, 1)

            def act_pass(j, p):
                for i in range(4):
                    act.wait_ge(up_drained, p * 8 + 2 * i + 1)
                    act.activation(sig_s[i % 2], glu_s[i % 2], ACT.Sigmoid, scale=ALPHA).then_inc(sigm_done, 1)
                    if i == 3:
                        hi(p, 1)
                    act.wait_ge(prod_done, p * 4 + i + 1)
                    act.activation(a_hi[:, 2 * i:2 * i + 2, 0:PASS], lin_s[i % 2], ACT.Copy).then_inc(ah_done, 1)
                    if i == 2:
                        hi(p, 0)
                hi(p, 2)
                hi(p, 3)
                for h in range(2):
                    act.wait_ge(pe_done, p * 12 + UP_CH + 2 * h + 2 + 4)
                    if h == 0:
                        act.wait_ge(given, p + 1)
                    for b, n in ((0, P), (1, PB)):
                        ins = act.activation(y_sb[j][b][:, h * 512:(h + 1) * 512], bank[4 + 2 * b + h][0:n, :], ACT.Copy,
                                             scale=idx[j][b][:, 2:3].bitcast(F32))
                    ins.then_inc(y_done, 1)

            act.wait_ge(over_done, 1)
            act.dma_start(over_dram, over_vi).then_inc(over_out, 16)
            act.wait_ge(over_out, 16)
            act.dma_start(over_row, over_dram.rearrange("(o q) f -> o (q f)", o=1)).then_inc(over_in, 16)
            act.wait_ge(over_in, 16)
            act.sem_inc(y_done, 2)
            act.wait_ge(h_ready, 2 * NTOK)
            with act.Fori(0, E_N // 2) as h:
                for j in range(2):
                    act_pass(j, h * 2 + j)
            n = act.value_load(over_row[0:1, 2:3], min_val=0, max_val=NOVER)
            with act.If(n > 0):
                with act.Fori(0, NOVER) as q:
                    with act.If(q < n):
                        act_pass(0, q + E_N)
            for t in range(NTOK):
                act.wait_ge(fin_sum, t + 1)
                if t >= 1:
                    act.wait_ge(fin_sq, t)
                act.activation(fin_junk, fin_h[t], ACT.Square, accum_out=fin_ss[:, t:t + 1]).then_inc(fin_sq, 1)
                act.wait_ge(fin_var, t + 1)
                act.activation(fin_r[:, t:t + 1], fin_v[:, t:t + 1], ACT.Sqrt).then_inc(fin_root, 1)
                act.wait_ge(fin_done, t + 1)
                act.dma_start(out_rows[t * P:(t + 1) * P, :], fin_h[t]).then_inc(stored, 16)

        def experts_dve(dve):
            step = dve_step

            def link(ins):
                step.mark(ins)
                dve.wait_ge(step.sem, step.now())

            dve.sem_inc(a_done, 2)
            dve.sem_inc(lo_done, 4)
            dve.wait_ge(mix_ready, 64)
            dve.wait_ge(merged, 16)
            for s in range(NTOK + 4):
                if s < NTOK:
                    t = s
                    dve.wait_ge(x_landed[t + 1], 32)
                    for c in range(2):
                        dve.wait_ge(h_ready, 2 * t + c + 1)
                        hh = h_rows[:, t, c * 512:(c + 1) * 512]
                        dve.tensor_tensor(hh, hh, bank[2 * (t % 2) + c][:, :], ALU.add).then_inc(h_added, 1)
                    ht = slice(t, t + 1)
                    dve.wait_ge(sq_done, t + 1)
                    dve.tensor_scalar(h_v[:, ht], h_ss[:, ht], 1.0 / D, EPS, ALU.mult, ALU.add).then_inc(v_done, 1)
                    dve.wait_ge(rt_done, t + 1)
                    link(dve.reciprocal(h_r[:, ht], h_r[:, ht]))
                    newton(dve, link, h_r[:, ht], h_v[:, ht], h_t[:, ht])
                    if t == 0:
                        dve.wait_ge(r_loads, 16 * 5)
                        dve.wait_ge(rc_done, 12)
                    if t >= 2:
                        dve.wait_ge(hf_stored[t % 2], 16 * (t // 2))
                        dve.wait_ge(hf_turned, 2 * (t - 1))
                    dve.scalar_tensor_tensor(hf_rows[t % 2], h_rows[:, t, :], h_r[:, ht], ffn_g, ALU.mult, ALU.mult).then_inc(hf_done, 1)
                if 2 <= s < NTOK + 2:
                    t = s - 2
                    dve.wait_ge(logits_ready, t + 1)
                    link(dve.tensor_tensor(logit[:, t, :], bank[6][:, 0:E_N], rout_b, ALU.add))
                    link(dve.max(top_v[:, t, :], logit[:, t, :]))
                    dve.tensor_scalar(ntop[:, t:t + 1], top_v[:, t, 0:1], -1.0, None, ALU.mult).then_inc(exp_in, 1)
                    link(dve.max_index(top_i[:, t, :], top_v[:, t, :], logit[:, t, :]))
                    link(dve.tensor_copy(top_e[:, t, :], top_i[:, t, 0:4]))
                    if t >= 2:
                        dve.wait_ge(slot_done, t - 1)
                    link(dve.tensor_tensor(pick[:, t % 2], bc(e_iota, 1, 4), bc(top_e[:, t, :], 2, E_N), ALU.is_equal))
                    link(dve.tensor_reduce(picked[:, t, :], pick[:, t % 2].rearrange("p k e -> p e k"), AX_X, ALU.add))
                    link(dve.tensor_tensor(running[:, t + 1, :], running[:, t, :], picked[:, t, :], ALU.add))
                    dve.wait_ge(exp_out, t + 1)
                    link(dve.reciprocal(esum[:, t:t + 1], esum[:, t:t + 1]))
                    link(dve.tensor_scalar(gate[:, t, :], expo[:, t, :], esum[:, t:t + 1], None, ALU.mult))
                    link(dve.tensor_copy(entry_f[:, t, :, 2], gate[:, t, :]))
                    link(dve.tensor_tensor(pick_g, pick[:, t % 2], bc(gate[:, t, :], 2, E_N), ALU.mult))
                    dve.tensor_reduce(gmat[:, t, :], pick_g.rearrange("p k e -> p e k"), AX_X, ALU.add).then_inc(picked_done, 1)
                if 3 <= s < NTOK + 3:
                    t = s - 3
                    dve.wait_ge(pos_ready, t + 1)
                    link(dve.tensor_tensor(place[:, t, :], bank[7][:, 0:E_N], e_region, ALU.add))
                    if t >= 2:
                        dve.wait_ge(bias_ready, 2 * t - 2)
                    dve.tensor_copy(gmat_T[:, t % 2, :], bank[7][0:E_N, P:2 * P]).then_inc(place_done, 1)
                    link(dve.tensor_tensor(pick_s, pick[:, t % 2], bc(place[:, t, :], 1, 4), ALU.mult))
                    link(dve.tensor_reduce(slot_f[:, t, :], pick_s, AX_X, ALU.add))
                    dve.tensor_copy(slot_i[:, 4 * t:4 * t + 4], slot_f[:, t, :]).then_inc(slot_done, 1)
                if s >= 4:
                    t = s - 4
                    for c in range(2):
                        dve.wait_ge(bias_ready, 2 * t + c + 1)
                        hh = h_rows[:, t, c * 512:(c + 1) * 512]
                        dve.tensor_tensor(hh, hh, bank[4 + c][:, :], ALU.add).then_inc(h2_added, 1)
            dve.wait_ge(counts_ready, 1)
            link(dve.tensor_copy(count_b, bank[6][:, 0:E_N]))
            for i in range(NI):
                step.mark(dve.tensor_scalar(flag[:, i * E_N:(i + 1) * E_N], count_b, float(PASS * (i + 1)), None, ALU.is_gt))
            dve.wait_ge(step.sem, step.now())
            link(dve.tensor_tensor_scan(cum, ones_f, flag, 0.0, ALU.mult, ALU.add))
            link(dve.tensor_scalar(sel_q, cum, over_q, None, ALU.is_equal))
            link(dve.tensor_tensor(sel_q, sel_q, flag, ALU.mult))
            link(dve.tensor_tensor(base_f, sel_q, base_f, ALU.mult))
            link(dve.tensor_tensor(exp_f, sel_q, exp_f, ALU.mult))
            link(dve.memset(over_v, 0.0))
            link(dve.tensor_reduce(over_v[:, 0:1], base_f, AX_X, ALU.add))
            link(dve.tensor_reduce(over_v[:, 1:2], exp_f, AX_X, ALU.add))
            link(dve.tensor_copy(over_v[:, 2:3], cum[:, NF - 1:NF]))
            link(dve.tensor_copy(over_v[0:E_N, 3:4], bank[6][0:E_N, E_N:E_N + 1]))
            dve.tensor_copy(over_vi, over_v).then_inc(over_done, 1)
            dve.wait_ge(bup_turned, 1)
            dve.tensor_copy(bias_T, bank[0][:, :]).then_inc(bup_done, 1)
            dve.wait_ge(bup_done, 1)

            def lo(p, d):
                dve.wait_ge(hi_done, p * 4 + d + 1)
                dve.tensor_tensor(w_lo[d], std((UP_CH + d) % RING), w_hi[d], ALU.subtract).then_inc(lo_done, 1)

            def store_x(j, p):
                for b in range(4):
                    dve.wait_ge(x_turned, p * 4 + b + 1)
                    dve.tensor_copy(x_T[j][:, 2 * b:2 * b + 2, :].rearrange("p a b -> p (a b)"), bank[b][:, 0:2 * PASS]).then_inc(x_stored, 1)

            def bounded(j, p, i, which, dst):
                c = 2 * i + which
                dve.wait_ge(pe_done, p * 12 + c + 1 + 4)
                src = bank[c % 4][:, 0:2 * PASS].rearrange("p (a b) -> p a b", b=PASS)
                for a in range(2):
                    f = which * 8 + 2 * i + a
                    ins = dve.tensor_scalar(dst[:, a, :], src[:, a, :], bias_now[j][:, f:f + 1], LIMIT, ALU.add, ALU.min)
                ins.then_inc(up_drained, 1)

            def a_low(p, i):
                dve.wait_ge(ah_done, p * 4 + i + 1)
                dve.tensor_tensor(a_lo[:, 2 * i:2 * i + 2, 0:PASS], lin_s[i % 2], a_hi[:, 2 * i:2 * i + 2, 0:PASS], ALU.subtract).then_inc(a_done, 1)

            def dve_pass(j, p, e, ahead):
                dve.tensor_copy(bias_now[j], bias_T[:, bass.ds(e * 16, 16)]).then_inc(bias_sem, 1)
                dve.wait_ge(bias_sem, p + 1)
                for i in range(4):
                    v = i % 2
                    dve.wait_ge(a_done, p * 4 + i + 1)
                    bounded(j, p, i, 0, glu_s[v])
                    if i >= 1:
                        a_low(p, i - 1)
                    if i == 3:
                        lo(p, 0)
                    bounded(j, p, i, 1, lin_s[v])
                    dve.wait_ge(up_drained, p * 8 + 2 * i + 2)
                    link(dve.tensor_scalar(lin_s[v], lin_s[v], -LIMIT, 1.0, ALU.max, ALU.add))
                    link(dve.tensor_tensor(lin_s[v], lin_s[v], glu_s[v], ALU.mult))
                    dve.wait_ge(sigm_done, p * 4 + i + 1)
                    dve.tensor_tensor(lin_s[v], lin_s[v], sig_s[v], ALU.mult).then_inc(prod_done, 1)
                a_low(p, 3)
                lo(p, 1)
                if ahead:
                    store_x(1 - j, p + 1)
                lo(p, 2)
                lo(p, 3)

            store_x(0, 0)
            link(dve.memset(a_hi[:, :, PASS:].bitcast(F32), 0.0))
            dve.memset(a_lo[:, :, PASS:].bitcast(F32), 0.0).then_inc(a_cleared, 1)
            with dve.Fori(0, E_N // 2 - 1) as h:
                step.enter(h, 16)
                for j in range(2):
                    p = h * 2 + j
                    dve_pass(j, p, p, True)
                step.leave(E_N // 2 - 1)
            dve_pass(0, E_N - 2, E_N - 2, True)
            dve_pass(1, E_N - 1, E_N - 1, False)
            dve.wait_ge(over_in, 16)
            n = dve.value_load(over_row[0:1, 2:3], min_val=0, max_val=NOVER)
            with dve.If(n > 0):
                with dve.Fori(0, NOVER) as q:
                    with dve.If(q < n):
                        e = dve.value_load(over_row[0:1, bass.ds(q * 4 + 1, 1)], min_val=0, max_val=E_N - 1)
                        store_x(0, q + E_N)
                        step.enter(q, 8)
                        dve_pass(0, q + E_N, e, False)
                        step.trip = None
            fs = Tally(fin_step)

            def flink(ins):
                fs.mark(ins)
                dve.wait_ge(fs.sem, fs.now())

            dve.wait_ge(fg_landed, 16)
            for s in range(NTOK + 1):
                if s < NTOK:
                    t = s
                    b = fin[t % FB]
                    dve.wait_ge(fin_landed[t % FB], 16 * (t // FB + 1))
                    flink(dve.tensor_tensor(b[:, 0:2, :], b[:, 0:2, :], b[:, 2:4, :], ALU.add))
                    flink(dve.tensor_tensor(b[:, 0, :], b[:, 0, :], b[:, 1, :], ALU.add))
                    dve.wait_ge(x_landed[t + 1], 48)
                    dve.tensor_tensor(fin_h[t], fin_h[t], b[:, 0, :], ALU.add).then_inc(fin_sum, 1)
                if s >= 1:
                    t = s - 1
                    ft = slice(t, t + 1)
                    dve.wait_ge(fin_sq, t + 1)
                    dve.tensor_scalar(fin_v[:, ft], fin_ss[:, ft], 1.0 / D, EPS, ALU.mult, ALU.add).then_inc(fin_var, 1)
                    dve.wait_ge(fin_root, t + 1)
                    flink(dve.reciprocal(fin_r[:, ft], fin_r[:, ft]))
                    newton(dve, flink, fin_r[:, ft], fin_v[:, ft], fin_t[:, ft])
                    dve.scalar_tensor_tensor(fin_h[t], fin_h[t], fin_r[:, ft], final_g, ALU.mult, ALU.mult).then_inc(fin_done, 1)

        def experts_pe(pe):
            pe.wait_ge(merged, 16)
            for u in range(64 - 8, 64):
                pe.wait_ge(mix_drained[u % 8], u // 8 + 1)
            for s in range(NTOK + 4):
                if s < NTOK:
                    t = s
                    for c in range(4):
                        if t == 0:
                            n = chunk_of[("out", c)]
                            pe.wait_ge(ring_landed[slot_of[n]], 16 * len(chunks_of_slot(n)))
                        if t >= 2 and c % 2 == 0:
                            pe.wait_ge(h_added, 2 * (t - 2) + c // 2 + 1)
                        w = slot(("out", c))
                        for k in range(KT):
                            ins = pe.matmul(bank[2 * (t % 2) + c // 2][:, (c % 2) * CH:(c % 2 + 1) * CH], m_T[:, k, t * P:(t + 1) * P], w[:, k, :],
                                            start=(k == 0), stop=(k == KT - 1))
                        if c % 2:
                            ins.then_inc(h_ready, 1)
                if 1 <= s <= NTOK:
                    t = s - 1
                    pe.wait_ge(hf_done, t + 1)
                    if t >= 1:
                        pe.wait_ge(hf_T_done, 2 * t)
                    if t >= 4:
                        pe.wait_ge(h2_added, 2 * (t - 4) + 2)
                    for c in range(2):
                        for a in range(4):
                            ins = pe.transpose(bank[4 + c][:, a * P:(a + 1) * P], hf_rows[t % 2][:, (4 * c + a) * P:(4 * c + a + 1) * P], ident)
                        ins.then_inc(hf_turned, 1)
                if 2 <= s < NTOK + 2:
                    t = s - 2
                    if t == 0:
                        pe.wait_ge(r_loads, 16 * 5)
                    pe.wait_ge(hf_T_done, 2 * t + 2)
                    if t >= 1:
                        pe.wait_ge(exp_in, t)
                    for k in range(KT):
                        ins = pe.matmul(bank[6][:, 0:E_N], hf_T[t % 2][:, k, :], rout_w[:, k, :], start=(k == 0), stop=(k == KT - 1))
                    ins.then_inc(logits_ready, 1)
                if 3 <= s < NTOK + 3:
                    t = s - 3
                    pe.wait_ge(picked_done, t + 1)
                    if t >= 1:
                        pe.wait_ge(place_done, t)
                    pe.matmul(bank[7][:, 0:E_N], before, picked[:, t, :], start=True, stop=False)
                    pe.matmul(bank[7][:, 0:E_N], ones, running[:, t, :], start=False, stop=True)
                    pe.transpose(bank[7][0:E_N, P:2 * P], gmat[:, t, :], ident).then_inc(pos_ready, 1)
                if s == NTOK + 2:
                    pe.matmul(bank[6][:, 0:E_N], ones, running[:, NTOK, :], start=True, stop=True)
                    pe.matmul(bank[6][0:E_N, E_N:E_N + 1], running[:, NTOK, :], ones[:, 0:1], start=True, stop=True).then_inc(counts_ready, 1)
                if s >= 4:
                    t = s - 4
                    pe.wait_ge(place_done, t + 1)
                    if s > NTOK:
                        pe.wait_ge(h2_added, 2 * t)
                    for c in range(2):
                        pe.wait_ge(hf_T_done, 2 * min(s, NTOK))
                        pe.matmul(bank[4 + c][:, :], gmat_T[:, t % 2, :], bdown[:, c * 512:(c + 1) * 512], start=True, stop=True).then_inc(bias_ready, 1)
            pe.wait_ge(h_added, 2 * NTOK)
            for a in range(4):
                ins = pe.transpose(bank[0][:, a * P:(a + 1) * P], raw_bias[:, a, :], ident)
            ins.then_inc(bup_turned, 1)
            pe.wait_ge(bup_done, 1)
            pe.wait_ge(h2_added, 2 * NTOK)
            pe.wait_ge(over_in, 16)

            def turn_x(j, p, uses):
                pe.wait_ge(gathered[j], uses * 32 + 32)
                for b in range(4):
                    if not (isinstance(p, int) and p == 0):
                        pe.wait_ge(up_drained, p * 8 + b - 3)
                    for a in range(2):
                        k = slice((2 * b + a) * P, (2 * b + a + 1) * P)
                        pe.transpose(bank[b][:, a * PASS:a * PASS + P], gat[j][0][:, k], ident)
                        ins = pe.transpose(bank[b][:, a * PASS + P:(a + 1) * PASS], gat[j][1][:, k], ident[0:PB, 0:PB])
                    ins.then_inc(x_turned, 1)

            def product(dst, left, right, first, last):
                pe.matmul(dst, left[0], right[0], start=first, stop=False)
                pe.matmul(dst, left[0], right[1], start=False, stop=False)
                return pe.matmul(dst, left[1], right[0], start=False, stop=last)

            def up(j, p, rows):
                for c in range(UP_CH):
                    landed(pe, p, c)
                    w = std(c % RING)
                    if c == 0:
                        pe.wait_ge(x_stored, p * 4 + 4)
                    if c >= 4:
                        pe.wait_ge(up_drained, p * 8 + c - 3)
                    for a in range(2):
                        f = slice(a * P, (a + 1) * P)
                        for k in range(KT):
                            ins = pe.matmul(bank[c % 4][:, a * PASS:a * PASS + rows], w[:, k, f], x_T[j][:, k, 0:rows],
                                            start=(k == 0), stop=(k == KT - 1))
                    ins.then_inc(pe_done, 1)

            def down(p, rows):
                for c in range(DN_CH):
                    pe.wait_ge(lo_done, p * 4 + c + 1 + 4)
                    if c % 2 == 0:
                        pe.wait_ge(y_done, p * 2 + c // 2 + 1)
                    for k in range(KT):
                        if c == 0 and k % 2 == 0:
                            pe.wait_ge(a_done, p * 4 + k // 2 + 1 + 2)
                        for b in range(1 if rows <= P else 2):
                            r = slice(b * P, (b + 1) * P)
                            ins = product(bank[4 + 2 * b + c // 2][:, (c % 2) * CH:(c % 2 + 1) * CH], (a_hi[:, k, r], a_lo[:, k, r]),
                                          (w_hi[c][:, k, :], w_lo[c][:, k, :]), k == 0, k == KT - 1)
                    ins.then_inc(pe_done, 1)

            def pe_pass(j, p, ahead):
                n = pe.value_load(over_row[0:1, bass.ds(p * 4 + 3, 1) if not isinstance(p, int) else slice(4 * p + 3, 4 * p + 4)], min_val=0, max_val=SEQ)
                with pe.If(n < P + 1):
                    up(j, p, P)
                with pe.If(n > P):
                    with pe.If(n < P + 17):
                        up(j, p, P + 16)
                    with pe.If(n > P + 16):
                        with pe.If(n < P + 33):
                            up(j, p, P + 32)
                        with pe.If(n > P + 32):
                            up(j, p, PASS)
                if ahead is not None:
                    turn_x(1 - j, p + 1, ahead)
                with pe.If(n < P + 1):
                    down(p, P)
                with pe.If(n > P):
                    down(p, PASS)

            pe.sem_inc(pe_done, 4)
            turn_x(0, 0, 0)
            pe.wait_ge(a_cleared, 1)
            with pe.Fori(0, E_N // 2 - 1) as h:
                for j in range(2):
                    pe_pass(j, h * 2 + j, h + j)
            pe_pass(0, E_N - 2, E_N // 2 - 1)
            pe_pass(1, E_N - 1, None)
            n = pe.value_load(over_row[0:1, 2:3], min_val=0, max_val=NOVER)
            with pe.If(n > 0):
                with pe.Fori(0, NOVER) as q:
                    with pe.If(q < n):
                        turn_x(0, q + E_N, q + E_N // 2)
                        up(0, q + E_N, PASS)
                        down(q + E_N, PASS)

        block = ctx.enter_context(nc.Block())

        @block.sync
        def _(sp):
            sp.dma_start(x_meta, meta_tokens).then_inc(x_landed[0], 16)
            for t in range(NTOK):
                sp.dma_start(x_in[t], x_rows[t * P:(t + 1) * P, :]).then_inc(x_landed[t + 1], 16)
            for n, src in enumerate(chunks):
                sl = slot_of[n]
                last = [m for m in range(n) if slot_of[m] == sl]
                if last:
                    sp.wait_ge(*used_when(last[-1]))
                for h, s in enumerate(src):
                    dst = std(sl) if len(src) == 1 else glu_view(sl)[:, h]
                    sp.dma_start(dst, s).then_inc(ring_landed[sl], 16)
            experts_sync(sp)

        @block.gpsimd
        def _(pool):
            cn = [0]

            def const(ins):
                ins.then_inc(consts_done, 1)
                cn[0] += 1

            def settle():
                pool.wait_ge(consts_done, cn[0])

            const(pool.memset(ident, 0.0))
            const(pool.memset(turn, 0.0))
            const(pool.memset(hide, 0.0))
            const(pool.memset(before, 1.0))
            const(pool.memset(ones, 1.0))
            const(pool.memset(sgn, 1.0))
            const(pool.memset(nsgn, 1.0))
            const(pool.memset(half_pi, math.pi / 2))
            const(pool.memset(spare, 0.0))
            const(pool.memset(ss, 1.0))
            const(pool.iota(step_j, [[1, NCH]], 0, 0, allow_small_or_imprecise_dtypes=True))
            const(pool.iota(step_t[:, 0:STEP], [[-1, STEP]], STEP - 1, 0, allow_small_or_imprecise_dtypes=True))
            const(pool.iota(step_t[:, STEP:2 * STEP], [[1, STEP]], 1, 0, allow_small_or_imprecise_dtypes=True))
            settle()
            sel = pool.affine_select
            const(sel(out=ident, in_=ident, compare_op=ALU.not_equal, fill=1.0, base=0, pattern=[[-1, P]], channel_multiplier=1))
            const(sel(out=turn[:, 0:P], in_=turn[:, 0:P], compare_op=ALU.not_equal, fill=1.0, base=0, pattern=[[-1, P]], channel_multiplier=1))
            const(sel(out=turn[:, P:P + NS], in_=turn[:, P:P + NS], compare_op=ALU.not_equal, fill=1.0, base=-NS, pattern=[[-1, NS]], channel_multiplier=1))
            const(sel(out=turn[:, P + NS:2 * P], in_=turn[:, P + NS:2 * P], compare_op=ALU.not_equal, fill=-1.0, base=0, pattern=[[-1, NS]], channel_multiplier=1))
            const(sel(out=before, in_=before, compare_op=ALU.is_gt, fill=0.0, base=0, pattern=[[1, P]], channel_multiplier=-1))
            const(sel(out=hide[:, 0:P], in_=hide[:, 0:P], compare_op=ALU.is_gt, fill=HIDE, base=0, pattern=[[1, P]], channel_multiplier=-1))
            const(sel(out=hide[:, P:2 * P], in_=hide[:, P:2 * P], compare_op=ALU.is_ge, fill=HIDE, base=0, pattern=[[-1, P]], channel_multiplier=1))
            const(sel(out=sgn, in_=sgn, compare_op=ALU.is_ge, fill=-1.0, base=NS - 1, pattern=[[0, 1]], channel_multiplier=-1))
            const(sel(out=nsgn, in_=nsgn, compare_op=ALU.is_ge, fill=-1.0, base=-NS, pattern=[[0, 1]], channel_multiplier=1))
            const(pool.memset(v_rows[:, 0, :], 0.0))
            settle()
            for k in k_T:
                const(pool.memset(k[0:HD, META:META + P], 0.0))
                settle()
                const(pool.memset(k[HD:HD + 1, :], 0.0))
                settle()
            settle()
            for k in k_T:
                const(pool.memset(k[HD:HD + 1, META:META + P], HIDE))
            settle()

            def move_u(ft):
                r = NXT + len(PIECES) * (ft + 1) - 1
                pool.wait_ge(pre_drained[r % 4], r // 4 + 1)
                pool.dma_start(u_dram[ft], u_T[ft % 2]).then_inc(u_out[ft], 16)
                pool.wait_ge(u_out[ft], 16)
                for s in range(STEP):
                    pool.dma_start(U[s * GC:(s + 1) * GC, 8 * ft:8 * ft + 8, :],
                                   u_dram[ft, :, s, :].rearrange("(g c) j -> c g j", c=GC)).then_inc(u_moved[ft], 16)

            for ft in range(4):
                move_u(ft)

            step = pool_step
            pool.wait_ge(par_done, 1)
            for i in range(NB):
                gs = slice(i * BG, (i + 1) * BG)
                if i >= 1:
                    pool.wait_ge(cs_done, 2 * i)
                jj = bc(step_j, 1, BG)
                step.mark(pool.tensor_tensor(Pa, jj, bc(hi8[:, gs], 2, NCH), ALU.mult))
                pool.wait_ge(step.sem, step.now())
                step.mark(pool.tensor_scalar(Pk, Pa, 1 / (2 * math.pi), MAGIC, ALU.mult, ALU.add))
                step.mark(pool.tensor_tensor(Pr, jj, bc(lo8[:, gs], 2, NCH), ALU.mult))
                pool.wait_ge(step.sem, step.now())
                step.mark(pool.tensor_scalar(Pk, Pk, MAGIC, -TWO_PI_HI, ALU.subtract, ALU.mult))
                pool.wait_ge(step.sem, step.now())
                step.mark(pool.tensor_tensor(Pa, Pa, Pk, ALU.add))
                pool.wait_ge(step.sem, step.now())
                step.mark(pool.tensor_tensor(Pa, Pa, Pr, ALU.add))
                step.mark(pool.tensor_scalar(Pk, Pk, TWO_PI_LO / TWO_PI_HI, None, ALU.mult))
                pool.wait_ge(step.sem, step.now())
                step.mark(pool.tensor_tensor(Pa, Pa, Pk, ALU.add))
                pool.wait_ge(step.sem, step.now())
                pool.tensor_scalar(Pr, Pa, 3.1415925, -3.1415925, ALU.min, ALU.max).then_inc(ang_ready, 1)
                if i >= 1:
                    pool.wait_ge(y_ready, i)
                pr, pi = (bc(t[:, gs, STEP:2 * STEP], 3, GC) for t in (ab_re, ab_im))
                k1, k2 = (bc(t[:, gs, :], 2, STEP) for t in (K1, K2))
                step.mark(pool.tensor_tensor(G1, pr, k1, ALU.mult))
                step.mark(pool.tensor_tensor(Gtmp, pi, k2, ALU.mult))
                pool.wait_ge(step.sem, step.now())
                step.mark(pool.tensor_tensor(G1, G1, Gtmp, ALU.add))
                step.mark(pool.tensor_tensor(G2, pr, k2, ALU.mult))
                pool.wait_ge(step.sem, step.now())
                step.mark(pool.tensor_tensor(Gtmp, pi, k1, ALU.mult))
                pool.wait_ge(step.sem, step.now())
                pool.tensor_tensor(G2, G2, Gtmp, ALU.subtract).then_inc(g_done, 1)

            pool.wait_ge(y_ready, NB)
            for q in q_blk:
                step.mark(pool.memset(q[HD:HD + 1], 1.0))
            pool.wait_ge(step.sem, step.now())
            r = NKV + 15
            pool.wait_ge(pre_drained[r % 4], r // 4 + 1)
            pool.sem_inc(q_staged, 1)
            with pool.Fori(0, NTOK // 2) as it:
                for half in range(2):
                    pool.wait_ge(s_ready, it * 32 + HEADS * (half + 1))
                    cs = bass.ds((it * 2 + half) * P, P)
                    for odd in range(2):
                        pool.wait_ge(q_staged, it * 4 + 2 * half + odd + 1)
                        pool.tensor_copy(q_blk[half][0:HD, odd:HEADS:2, :], q_T[odd * HD:(odd + 1) * HD, :, cs]).then_inc(q_staged, 1)
            experts_pool(pool)

        @block.scalar
        def _(act):
            act.dma_start(mix_g, mix_norm_g.rearrange("l (k p) -> p (l k)", p=P), allow_slow_non_contiguous=True).then_inc(g_landed, 16)
            act.dma_start(sinks, attn_sinks.partition_broadcast(P).rearrange("p l h -> p (l h)")).then_inc(g_landed, 16)
            sq = lambda a: a.rearrange("l a b -> (l a) b")
            par = []
            for h in range(2):
                par.append((raw_ar[:, h * NS:(h + 1) * NS], sq(ssm_a_re)))
                par.append((raw_ai[:, h * NS:(h + 1) * NS], sq(ssm_a_im)))
            par.append((raw_dt, ssm_log_dt.partition_broadcast(P).rearrange("p l g -> p (l g)")))
            for n, s in enumerate((ssm_b_re, ssm_b_im)):
                s = s.rearrange("l g p c -> p (l g) c")
                par.append((raw_b1[n * NS:(n + 1) * NS], s))
                par.append((raw_b2[(1 - n) * NS:(2 - n) * NS], s))
            for n, s in enumerate((ssm_c_re, ssm_c_im)):
                s = s.rearrange("l (a g) c p -> (g c) (l a) p", a=4)
                par.append((raw_c1[:, :, n * NS:(n + 1) * NS], s))
                par.append((raw_c2[:, :, (1 - n) * NS:(2 - n) * NS], s))
            for s in range(STEP):
                par.append((raw_d[:, s, :], ssm_d.rearrange("l (g c) -> (l g) c", c=GC)))
            act.wait_ge(consts_done, 10)
            for t in range(NTOK + 1):
                n = META if t == 0 else P
                act.wait_ge(x_landed[t], 16)
                if t >= 1:
                    act.wait_ge(squares_done, t)
                act.activation(junk[0:n], x_meta if t == 0 else x_in[t - 1], ACT.Square,
                               accum_out=ss[0:n, t:t + 1]).then_inc(squares_done, 1)
            act.wait_ge(var_done, 1)
            act.activation(rstd, nw1, ACT.Sqrt).then_inc(root_done, 1)
            for dst, src in par:
                act.dma_start(dst, src).then_inc(par_landed, 16)
            r = NXT
            for ft in range(4):
                if ft == 1:
                    act.wait_ge(par_landed, 16 * len(par))
                    act.activation(dt_, raw_dt, ACT.Exp).then_inc(dt_done, 1)
                if ft == 2:
                    act.wait_ge(pow_ready, 1)
                    act.activation(ph[0], ph[0], ACT.Exp).then_inc(pow_done, 1)
                    act.activation(ph[1], ph[1], ACT.Sin).then_inc(pow_done, 1)
                    act.activation(ph[2], ph[2], ACT.Sin, bias=half_pi, scale=-1.0).then_inc(pow_done, 1)
                if ft >= 2:
                    act.wait_ge(u_out[ft - 2], 16)
                for c0, n in PIECES:
                    act.wait_ge(pre_ready, r + 1)
                    act.activation(u_T[ft % 2][:, :, c0 // STEP:(c0 + n) // STEP],
                                   pre_bank(r)[:, 0:n].rearrange("p (j s) -> p s j", s=STEP), ACT.Copy)\
                       .then_inc(pre_drained[r % 4], 1)
                    r += 1
            for c0, n, d0 in ((0, META, 0), (0, 512, META + P), (512, 512, META + P + 512)):
                act.wait_ge(pre_ready, r + 1)
                for h in range(2):
                    ins = act.activation(k_T[h][0:HD, d0:d0 + n], pre_bank(r)[h * HD:(h + 1) * HD, 0:n], ACT.Copy)
                ins.then_inc(pre_drained[r % 4], 1)
                r += 1
            act.wait_ge(pre_ready, r + 1)
            act.activation(v_meta[0:META], pre_bank(r)[0:META, 0:P], ACT.Copy).then_inc(pre_drained[r % 4], 1)
            r += 1
            for h in range(2):
                act.wait_ge(pre_ready, r + 1)
                act.activation(v_rows[:, 1 + 4 * h:5 + 4 * h, :].rearrange("p a b -> p (a b)"), pre_bank(r)[:, :], ACT.Copy)\
                   .then_inc(pre_drained[r % 4], 1)
                r += 1

            def queries(n, r):
                act.wait_ge(pre_ready, r + 1)
                act.activation(q_T[:, n // 2, (n % 2) * 512:(n % 2 + 1) * 512], pre_bank(r)[:, :], ACT.Copy,
                               scale=-1.0 / 8).then_inc(pre_drained[r % 4], 1)

            def fetch_y(ft):
                act.dma_start(y_T[:, ft], y_dram[ft]).then_inc(y_moved[ft], 16)

            def outputs(i):
                act.wait_ge(y_ready, i + 1)
                if i >= 2 and i % 2 == 0:
                    act.wait_ge(y_out[i // 2 - 1], 16 * STEP)
                    fetch_y(i // 2 - 1)
                act.activation(Ysb[:, (i % 2) * BG:(i % 2 + 1) * BG, :].rearrange("p a b -> p (a b)"), bank[0][:, :], ACT.Copy)\
                   .then_inc(y_drained, 1)
                if i % 2:
                    ft = i // 2
                    act.wait_ge(y_drained, i + 1)
                    if i == 1:
                        for f in (2, 3):
                            act.wait_ge(u_out[f], 16)
                    for s in range(STEP):
                        act.dma_start(y_dram[ft, :, s, :].rearrange("(g c) j -> c g j", c=GC),
                                      Ysb[s * GC:(s + 1) * GC, :, :]).then_inc(y_out[ft], 16)

            for i in range(NB):
                queries(2 * i, r + 2 * i)
                act.wait_ge(ang_ready, i + 1)
                if i >= 1:
                    act.wait_ge(pq_done, i)
                act.activation(Pk, Pr, ACT.Abs).then_inc(abs_done, 1)
                act.activation(Sj, Pr, ACT.Sin).then_inc(cs_done, 1)
                act.wait_ge(abs_done, i + 1)
                act.activation(Cj, Pk, ACT.Sin, bias=half_pi, scale=-1.0).then_inc(cs_done, 1)
                if i >= 1:
                    outputs(i - 1)
                queries(2 * i + 1, r + 2 * i + 1)
            outputs(NB - 1)
            act.wait_ge(y_out[3], 16 * STEP)
            fetch_y(3)
            for ft in range(4):
                act.wait_ge(y_moved[ft], 16)
            for ft in range(4):
                act.activation(gy_T[:, ft, :].rearrange("p (j s) -> p s j", s=STEP), y_T[:, ft],
                               ACT.Gelu_apprx_tanh).then_inc(gelu_done, 1)
            act_attention(act)
            act_merge(act)
            experts_act(act)

        @block.vector
        def _(dve):
            step = dve_step

            def link(ins):
                step.mark(ins)
                dve.wait_ge(step.sem, step.now())

            dve.wait_ge(consts_done, 22)
            dve.wait_ge(g_landed, 32)
            dve.wait_ge(squares_done, NTOK + 1)
            link(dve.tensor_scalar(nw1, ss, 1.0 / D, EPS, ALU.mult, ALU.add))
            dve.memset(nw2, 0.0).then_inc(var_done, 1)
            dve.wait_ge(root_done, 1)
            link(dve.reciprocal(rstd, rstd))
            newton(dve, link, rstd, nw1, nw2)
            for t in range(NTOK + 1):
                v, n = (x_meta, META) if t == 0 else (x_in[t - 1], P)
                dve.tensor_scalar(v, v, rstd[0:n, t:t + 1], None, ALU.mult).then_inc(hn_rows_done, 1)
            for r in range(NXT):
                dve.wait_ge(pre_ready, r + 1)
                if r == 0:
                    dst, src, g = hn_T[:, :, 0:META], pre_bank(r)[:, 0:KT * META].rearrange("p (k n) -> p k n", n=META), bc(mix_g, 2, META)
                else:
                    t, c = divmod(r - 1, 2)
                    dst = hn_T[:, 4 * c:4 * c + 4, META + t * P:META + (t + 1) * P]
                    src, g = pre_bank(r)[:, :].rearrange("p (k n) -> p k n", n=P), bc(mix_g[:, 4 * c:4 * c + 4], 2, P)
                dve.tensor_tensor(dst, src, g, ALU.mult).then_inc(pre_drained[r % 4], 1)

            dve.wait_ge(par_turned, 3)
            link(dve.tensor_copy(a_re, bank[0][:, 0:G]))
            link(dve.tensor_copy(a_im, bank[0][:, G:2 * G]))
            link(dve.tensor_copy(skip_d, bank[0][:, 2 * G:3 * G]))
            k1f, k2f = (t.rearrange("p a b -> p (a b)") for t in (K1, K2))
            link(dve.tensor_scalar(k1f, bank[1][:, :], sgn, None, ALU.mult))
            link(dve.tensor_scalar(k2f, bank[2][:, :], -1.0, None, ALU.mult))
            link(dve.tensor_scalar(raw_b2, raw_b2, nsgn, None, ALU.mult))
            dve.wait_ge(dt_done, 1)
            link(dve.tensor_tensor(zz, a_re, dt_, ALU.mult))
            link(dve.tensor_tensor(c1, a_im, dt_, ALU.mult))

            def less_turns(r, ang, k):
                link(dve.tensor_scalar(k, ang, 1 / (2 * math.pi), MAGIC, ALU.mult, ALU.add))
                link(dve.tensor_scalar(k, k, MAGIC, None, ALU.subtract))
                link(dve.scalar_tensor_tensor(r, k, -TWO_PI_HI, ang, ALU.mult, ALU.add))
                link(dve.scalar_tensor_tensor(r, k, -TWO_PI_LO, r, ALU.mult, ALU.add))

            def split(hi, lo, r):
                link(dve.tensor_scalar(hi, r, SPLIT, None, ALU.add))
                link(dve.tensor_scalar(hi, hi, SPLIT, None, ALU.subtract))
                link(dve.tensor_tensor(lo, r, hi, ALU.subtract))

            less_turns(thr, c1, c2)
            split(hi1, lo1, thr)
            tt = bc(step_t, 1, G)
            link(dve.tensor_tensor(ph[0], tt, bc(zz, 2, 2 * STEP), ALU.mult))
            link(dve.tensor_tensor(ph[1], tt, bc(hi1, 2, 2 * STEP), ALU.mult))
            link(dve.tensor_tensor(ph[2], tt, bc(lo1, 2, 2 * STEP), ALU.mult))
            link(dve.tensor_scalar(ph[3], ph[1], 1 / (2 * math.pi), MAGIC, ALU.mult, ALU.add))
            link(dve.tensor_scalar(ph[3], ph[3], MAGIC, None, ALU.subtract))
            link(dve.scalar_tensor_tensor(ph[1], ph[3], -TWO_PI_HI, ph[1], ALU.mult, ALU.add))
            link(dve.tensor_tensor(ph[1], ph[1], ph[2], ALU.add))
            link(dve.scalar_tensor_tensor(ph[1], ph[3], -TWO_PI_LO, ph[1], ALU.mult, ALU.add))
            link(dve.tensor_copy(c1, ph[1][:, :, 2 * STEP - 1]))
            link(dve.tensor_scalar(ph[2], ph[1], -1.0, None, ALU.mult))
            link(dve.tensor_tensor(ph[2], ph[2], ph[1], ALU.max))
            dve.tensor_scalar(ph[1], ph[1], 3.1415925, -3.1415925, ALU.min, ALU.max).then_inc(pow_ready, 1)
            split(hi8, lo8, c1)
            dve.wait_ge(pow_done, 3)
            link(dve.tensor_tensor(ab_re, ph[0], ph[2], ALU.mult))
            link(dve.tensor_tensor(ab_im, ph[0], ph[1], ALU.mult))
            link(dve.tensor_tensor(c1, a_re, a_re, ALU.mult))
            link(dve.tensor_tensor(c2, a_im, a_im, ALU.mult))
            link(dve.tensor_scalar(c3, ab_re[:, :, STEP], 1.0, None, ALU.subtract))
            link(dve.tensor_tensor(c1, c1, c2, ALU.add))
            link(dve.reciprocal(thr, c1))
            link(dve.tensor_tensor(c1, c3, a_re, ALU.mult))
            link(dve.tensor_tensor(c2, ab_im[:, :, STEP], a_im, ALU.mult))
            link(dve.tensor_tensor(c1, c1, c2, ALU.add))
            link(dve.tensor_tensor(c1, c1, thr, ALU.mult))
            link(dve.tensor_tensor(c2, ab_im[:, :, STEP], a_re, ALU.mult))
            link(dve.tensor_tensor(c4, c3, a_im, ALU.mult))
            link(dve.tensor_tensor(c2, c2, c4, ALU.subtract))
            link(dve.tensor_tensor(c2, c2, thr, ALU.mult))
            cre, cim = bc(c1, 2, GC), bc(c2, 2, GC)
            p3, p4 = ph[3], ph[4]
            link(dve.tensor_tensor(B1, cre, raw_b1, ALU.mult))
            link(dve.tensor_tensor(p3, cim, raw_b2, ALU.mult))
            link(dve.tensor_tensor(B2, cre, raw_b2, ALU.mult))
            link(dve.tensor_tensor(p4, cim, raw_b1, ALU.mult))
            link(dve.tensor_tensor(B1, B1, p3, ALU.add))
            link(dve.tensor_tensor(B2, B2, p4, ALU.subtract))
            link(dve.tensor_scalar(nsinks, sinks, -1.0, None, ALU.mult))
            link(dve.memset(Wrev[:, :, STEP:, :], 0.0))
            dve.tensor_copy(c3, ph[0][:, :, 2 * STEP - 1]).then_inc(par_done, 1)

            def matrices(i):
                gs = slice(i * BG, (i + 1) * BG)
                if i >= 1:
                    dve.wait_ge(et_ready, BG * i)
                step.mark(dve.tensor_tensor(Wrev[:, :, 0:STEP, :], bc(ab_re[:, gs, 0:STEP], 3, GC), bc(B1[:, gs, :], 2, STEP), ALU.mult))
                link(dve.tensor_tensor(Wtmp, bc(ab_im[:, gs, 0:STEP], 3, GC), bc(B2[:, gs, :], 2, STEP), ALU.mult))
                dve.tensor_tensor(Wrev[:, :, 0:STEP, :], Wrev[:, :, 0:STEP, :], Wtmp, ALU.add).then_inc(w_done, 1)

            dve.wait_ge(par_done, 1)
            matrices(0)
            for i in range(NB):
                for g in range(BG):
                    n = i * BG + g
                    dve.wait_ge(et_ready, n + 1)
                    if i >= 1 and g == 0:
                        dve.wait_ge(y_ready, i)
                    b = bank[g % 2]
                    step.mark(dve.tensor_copy(ET[:, g, 0:2 * P], b[:, 0:2 * P]))
                    dve.scalar_tensor_tensor(ET[:, g, 2 * P:3 * P], ident, skip_d[:, n:n + 1], b[:, 2 * P:3 * P],
                                             ALU.mult, ALU.add).then_inc(et_drained, 1)
                step.mark(dve.tensor_copy(decay, bc(c3[:, i * BG:(i + 1) * BG], 2, NCH)))
                dve.wait_ge(step.sem, step.now())
                step.mark(dve.memset(decay[:, :, 0:1], 0.0))
                if i + 1 < NB:
                    matrices(i + 1)
                dve.wait_ge(cs_done, 2 * i + 2)
                for pr in range(2):
                    dve.wait_ge(xs_ready, 2 * i + pr + 1)
                    gg = slice(2 * pr, 2 * pr + 2)
                    xr, xi = (bank[2 + q][:, 0:2 * NCH].rearrange("p (a b) -> p a b", b=NCH) for q in range(2))
                    step.mark(dve.tensor_tensor(Wj[:, gg, :], Cj[:, gg, :], xr, ALU.mult))
                    link(dve.tensor_tensor(Vj[:, gg, :], Sj[:, gg, :], xi, ALU.mult))
                    dve.tensor_tensor(Wj[:, gg, :], Wj[:, gg, :], Vj[:, gg, :], ALU.add).then_inc(xs_drained, 1)
                dve.wait_ge(xs_drained, 2 * i + 2)
                flat = lambda t: t.rearrange("p a b -> p (a b)")
                link(dve.tensor_tensor_scan(flat(Vj), flat(decay), flat(Wj), 0.0, ALU.mult, ALU.add))
                if i >= 1:
                    dve.wait_ge(y_ready, i)
                js = slice(MCH - 1, NCH - 1)
                step.mark(dve.tensor_tensor(Pj, Cj[:, :, js], Vj[:, :, js], ALU.mult))
                dve.tensor_tensor(Qj, Sj[:, :, js], Vj[:, :, js], ALU.mult).then_inc(pq_done, 1)
            dve_attention(dve, step, link)
            dve_merge(dve, step)
            experts_dve(dve)

        @block.tensor
        def _(pe):
            def take(name):
                n = chunk_of[name]
                pe.wait_ge(ring_landed[slot_of[n]], 16 * len(chunks_of_slot(n)))

            pe.wait_ge(consts_done, 22)
            def group(r):
                if r >= 4:
                    pe.wait_ge(pre_drained[r % 4], r // 4)
                return pre_bank(r)

            for r in range(NXT):
                t, c = (0, 0) if r == 0 else (1 + (r - 1) // 2, (r - 1) % 2)
                pe.wait_ge(hn_rows_done, t + 1)
                b = group(r)
                for k in range(KT if r == 0 else 4):
                    if r == 0:
                        ins = pe.transpose(b[:, k * META:(k + 1) * META], x_meta[:, k * P:(k + 1) * P], ident[0:META, 0:META])
                    else:
                        kk = 4 * c + k
                        ins = pe.transpose(b[:, k * P:(k + 1) * P], x_in[t - 1][:, kk * P:(kk + 1) * P], ident)
                ins.then_inc(pre_ready, 1)
            pe.wait_ge(pre_drained[(NXT - 1) % 4], (NXT - 1) // 4 + 1)

            pe.wait_ge(par_landed, 16 * 21)
            pe.transpose(bank[0][:, 0:G], raw_ar, ident[0:G, 0:G])
            pe.transpose(bank[0][:, G:2 * G], raw_ai, ident[0:G, 0:G])
            pe.transpose(bank[0][:, 2 * G:3 * G], raw_d.rearrange("p a b -> p (a b)"), ident[0:G, 0:G]).then_inc(par_turned, 1)
            for n, raw in ((1, raw_c1), (2, raw_c2)):
                for a in range(4):
                    ins = pe.transpose(bank[n][:, a * P:(a + 1) * P], raw[:, a, :], ident)
                ins.then_inc(par_turned, 1)

            def project(r, w, c0, n, rhs):
                b = group(r)
                for k in range(KT):
                    ins = pe.matmul(b[:, 0:n], w[:, k, :], rhs[:, k, c0:c0 + n], start=(k == 0), stop=(k == KT - 1))
                ins.then_inc(pre_ready, 1)
                return ins

            r = NXT
            for ft in range(4):
                take(("u", ft // 2))
                for c0, n in PIECES:
                    project(r, slot(("u", ft // 2))[:, :, (ft % 2) * P:(ft % 2 + 1) * P], c0, n, hn_T)
                    r += 1
            take("kv")
            w = slot("kv")
            for c0, n in ((0, META), (META, 512), (META + 512, 512)):
                project(r, w[:, :, 0:P], c0, n, hn_T)
                r += 1
            b = group(r)
            for k in range(KT):
                ins = pe.matmul(b[0:META, 0:P], hn_T[:, k, 0:META], w[:, k, P:2 * P], start=(k == 0), stop=(k == KT - 1))
            ins.then_inc(pre_ready, 1)
            r += 1
            for h in range(2):
                b = group(r)
                for t in range(4):
                    c0 = META + (4 * h + t) * P
                    for k in range(KT):
                        ins = pe.matmul(b[:, t * P:(t + 1) * P], hn_T[:, k, c0:c0 + P], w[:, k, P:2 * P], start=(k == 0), stop=(k == KT - 1))
                ins.then_inc(pre_ready, 1)
                r += 1

            def queries(n, ks=range(KT)):
                ft, h = divmod(n, 2)
                if 0 in ks:
                    take(("q", ft // 2))
                    group(NKV + n)
                for k in ks:
                    ins = pe.matmul(pre_bank(NKV + n)[:, :], slot(("q", ft // 2))[:, k, (ft % 2) * P:(ft % 2 + 1) * P],
                                    hn_T[:, k, META + h * 512:META + (h + 1) * 512], start=(k == 0), stop=(k == KT - 1))
                if KT - 1 in ks:
                    ins.then_inc(pre_ready, 1)

            def matrices(i):
                pe.wait_ge(w_done, i + 1)
                for g in range(BG):
                    n = i * BG + g
                    b = bank[g % 2]
                    if n >= 2:
                        pe.wait_ge(et_drained, n - 1)
                    if i >= 1 and g == 0:
                        pe.wait_ge(y_drained, i)
                    wf = Wrev[:, g].rearrange("p m c -> p (m c)")
                    pe.matmul(b[:, 0:2 * P], wf[:, 0:P], turn, start=True, stop=True)
                    for t in range(STEP):
                        a = (STEP - 1 - t) * GC
                        ins = pe.matmul(b[:, 2 * P + t * GC:2 * P + (t + 1) * GC], wf[:, a:a + P], K1[:, n, :], start=True, stop=True)
                    ins.then_inc(et_ready, 1)
                    queries(2 * i + 1, range(g * KT // BG, (g + 1) * KT // BG))

            def chunk_inputs(i):
                for pr in range(2):
                    pe.wait_ge(et_drained, i * BG + 2 * pr + 2)
                    if 2 * i + pr >= 1:
                        pe.wait_ge(xs_drained, 2 * i + pr)
                    if i % 2 == 0 and pr == 0:
                        pe.wait_ge(u_moved[i // 2], 16 * STEP)
                    for g in (2 * pr, 2 * pr + 1):
                        n = i * BG + g
                        for q in range(2):
                            ins = pe.matmul(bank[2 + q][:, (g % 2) * NCH:(g % 2 + 1) * NCH], ET[:, g, q * P:(q + 1) * P], U[:, n, :], start=True, stop=True)
                    ins.then_inc(xs_ready, 1)

            def outputs(i):
                pe.wait_ge(pq_done, i + 1)
                pe.wait_ge(g_done, i + 1)
                pe.wait_ge(et_drained, (i + 1) * BG)
                for g in range(BG):
                    n = i * BG + g
                    o = bank[0][:, g * P:(g + 1) * P]
                    pe.matmul(o, ET[:, g, 2 * P:3 * P], U[:, n, MCH:NCH], start=True, stop=False)
                    pe.matmul(o, G1[:, g].rearrange("p t c -> p (t c)"), Pj[:, g, :], start=False, stop=False)
                    ins = pe.matmul(o, G2[:, g].rearrange("p t c -> p (t c)"), Qj[:, g, :], start=False, stop=True)
                ins.then_inc(y_ready, 1)

            for i in range(NB):
                queries(2 * i)
                if i >= 1:
                    outputs(i - 1)
                matrices(i)
                chunk_inputs(i)
            outputs(NB - 1)

            pe.sem_inc(s_ready, 32)
            pe.sem_inc(pt_turned, 2)
            pe.sem_inc(pt_used, 2)
            pe.sem_inc(at_ready, 4)
            for r in range(NKV + 12, NKV + 16):
                pe.wait_ge(pre_drained[r % 4], r // 4 + 1)
            pe.wait_ge(consts_done, 29)
            pe.wait_ge(y_drained, NB)
            gs_before = 16 * len(chunks_of_slot(chunk_of[("gs", 0)])) - 16
            with pe.Fori(0, NTOK // 2) as it:
                def turn_back(half):
                    pe.wait_ge(o_rows, it * 4 + 2 * half + 2 + 2)
                    pe.wait_ge(gs_done, it * 4 + 3 + half)
                    for c in range(2):
                        pe.wait_ge(at_free, it * 4 + 2 * half + c + 1)
                        for a in range(4):
                            f = o_sb[half].rearrange("p h d -> p (h d)")[:, (4 * c + a) * P:(4 * c + a + 1) * P]
                            ins = pe.transpose(bank[6 + c][:, a * P:(a + 1) * P], f, ident)
                        ins.then_inc(at_ready, 1)

                for i in range(32 + 3):
                    if i < 32:
                        half, h = divmod(i, HEADS)
                        if h == 0:
                            pe.wait_ge(q_staged, it * 4 + 2 * half + 2 + 1)
                        k = k_T[h // REP]
                        q = q_blk[half][0:HD + 1, h, :]
                        pe.wait_ge(s_done, it * 32 + i + 1)
                        pe.matmul(bank[i % 2][:, 0:2 * P], q, k[0:HD + 1, bass.ds((it * 2 + half) * P + META, 2 * P)], start=True, stop=True)
                        pe.matmul(bank[i % 2][:, 2 * P:2 * P + META], q, k[0:HD + 1, 0:META], start=True, stop=True).then_inc(s_ready, 1)
                    for n, k in GS_STEPS[i]:
                        if k == 0:
                            if n == 0:
                                pe.wait_ge(ring_landed[RING - 1], it * 16 + gs_before + 16)
                            if n == 2:
                                pe.wait_ge(gs_done, it * 4 + 1)
                            else:
                                pe.wait_ge(at_free, it * 4 + (4 if n == 3 else 2))
                        ins = pe.matmul(bank[6 + n % 2][:, :], slot(("gs", 0))[:, k, (n // 2) * P:(n // 2 + 1) * P],
                                        hn_T[:, k, META + (n % 2) * 512:META + (n % 2 + 1) * 512], start=(k == 0), stop=(k == KT - 1))
                        if k == KT - 1:
                            ins.then_inc(gs_ready, 1)
                    if 2 <= i < 34:
                        j = i - 2
                        pe.wait_ge(p_done, it * 32 + j + 1 + 2)
                        pe.wait_ge(pt_a, it * 32 + j + 1)
                        pe.wait_ge(pt_b, it * 32 + j + 1)
                        for a in range(2):
                            pe.transpose(bank[2 + j % 2][:, a * P:(a + 1) * P], p_sb[j % 2][:, a * P:(a + 1) * P], ident)
                        pe.transpose(bank[2 + j % 2][0:META, 2 * P:3 * P], p_sb[j % 2][:, 2 * P:2 * P + META], ident).then_inc(pt_turned, 1)
                    if i >= 3:
                        j = i - 3
                        half, h = divmod(j, HEADS)
                        g = h // REP
                        pe.wait_ge(pt_a, it * 32 + j + 1 + 2)
                        pe.wait_ge(pt_b, it * 32 + j + 1 + 2)
                        if h % REP == 0:
                            pe.wait_ge(o_rows, it * 4 + j // REP + 1)
                        o = bank[4 + g % 2][:, (h % REP) * HD:(h % REP + 1) * HD]
                        for a in range(2):
                            pe.matmul(o, pt_sb[j % 2][:, a * P:(a + 1) * P],
                                      v_rows[:, bass.ds(it * 2 + half + a, 1), g * HD:(g + 1) * HD].rearrange("p a d -> p (a d)"), start=(a == 0), stop=False)
                        ins = pe.matmul(o, pt_sb[j % 2][0:META, 2 * P:3 * P], v_meta[0:META, g * HD:(g + 1) * HD], start=False, stop=True)
                        ins.then_inc(pt_used, 1)
                    if i == 24:
                        turn_back(0)
                turn_back(1)

            pe.wait_ge(gelu_done, 4)
            pe.wait_ge(at_free, 2 * NTOK + 2)
            for c in range(4):
                for kind, (name, rhs, c0) in enumerate(((("glu", c), gy_T, 0), (("glu", c), gy_T, 0),
                                                        (("ga", c), hn_T, META), (("ao", c), q_T, 0))):
                    take(name)
                    s = slot_of[chunk_of[name]]
                    for g in range(4):
                        u = c * 16 + kind * 4 + g
                        if u >= 8:
                            pe.wait_ge(mix_drained[u % 8], u // 8)
                        w = glu_view(s)[:, 1 - kind] if name[0] == "glu" else std(s)
                        kt = w.shape[1]
                        f = (g // 2) * P
                        for k in range(kt):
                            ins = pe.matmul(bank[u % 8][:, :], w[:, k, f:f + P], rhs[:, k, c0 + (g % 2) * 512:c0 + (g % 2 + 1) * 512],
                                            start=(k == 0), stop=(k == kt - 1))
                        ins.then_inc(mix_ready, 1)
            experts_pe(pe)


_INS = ['x', 'meta_tokens', 'mix_norm_g', 'w_in', 'ssm_a_re', 'ssm_a_im', 'ssm_log_dt', 'ssm_b_re', 'ssm_b_im',
        'ssm_c_re', 'ssm_c_im', 'ssm_d', 'w_ssm_glu', 'attn_sinks', 'w_attn_o', 'w_out', 'ffn_norm_g',
        'router_w', 'router_b', 'w_up', 'b_up', 'w_down', 'b_down', 'final_norm_g']
_OUTS = [((1, 1024, 1024), 'float32')]


def kernel(**inputs):
    import numpy as _np
    import concourse.bacc as _bacc
    from concourse import mybir as _mybir
    from concourse.bass_utils import run_bass_kernel_spmd as _run

    nc = _bacc.Bacc("TRN2", target_bir_lowering=False, num_devices=1)
    arrays, args = {}, []
    for name in _INS:
        a = _np.ascontiguousarray(inputs[name])
        arrays[f"in_{name}_dram"] = a
        args.append(nc.dram_tensor(f"in_{name}_dram", a.shape, _mybir.dt.from_np(a.dtype), kind="ExternalInput").ap())
    for i, (shape, dtype) in enumerate(_OUTS):
        dt = _mybir.dt.from_np(_np.dtype(dtype))
        args.append(nc.dram_tensor(f"out_{i}_dram", shape, dt, kind="ExternalOutput").ap())
    build_trunk(nc, *args)
    r = _run(nc, [arrays], core_ids=[0])
    return r.results[0]["out_0_dram"]
```
